# Optimizing a Trainium2 kernel written in Bass

```python
import math
import jax, jax.numpy as jnp
from jax import lax
import numpy as np

D_MODEL = 1024
BATCH = 1
SEQ = 256
DEPTH = 2

HEAD_DIM = 64
BRANCH_WIDTH = D_MODEL // 2
MIX_WIDTH = 2 * BRANCH_WIDTH
IN_WIDTH = 4 * MIX_WIDTH
N_HEADS_A = BRANCH_WIDTH // (2 * HEAD_DIM)
N_HEADS_B = BRANCH_WIDTH // HEAD_DIM
N_HEADS_C = BRANCH_WIDTH // HEAD_DIM
N_HEADS_D = BRANCH_WIDTH // HEAD_DIM
DIL_PAIRS = ((128, 1), (512, 4), (2048, 16))
MOBA_BLOCK = 256
MOBA_TOPK = 3
MOBA_CHUNK = 32
Q_BLOCK = 128
N_EVEN = (DEPTH + 1) // 2
N_ODD = DEPTH // 2
EPS = 1e-6
NEG_INF = -1e30

kernel_name = 'hybrid_diff_dilated_moba_stickbreak'

def rms_norm(x, w):
    xf = x.astype(jnp.float32)
    y = xf * lax.rsqrt(jnp.mean(xf * xf, axis=-1, keepdims=True) + EPS)
    return (y * w.astype(jnp.float32)).astype(x.dtype)

def alibi_slopes(n):
    return jnp.asarray(np.array([2.0 ** (-8.0 * (h + 1) / n) for h in range(n)], np.float32))

def split_heads(t, n):
    b, s, _ = t.shape
    return t.reshape(b, s, n, -1).transpose(0, 2, 1, 3)

def merge_heads(t):
    b, h, s, d = t.shape
    return t.transpose(0, 2, 1, 3).reshape(b, s, h * d)

def unblock(o):
    nb, b, h, blk, d = o.shape
    return o.transpose(1, 2, 0, 3, 4).reshape(b, h, nb * blk, d)

def diff_attention(q, k, v, q_norm, k_norm, lam, subln, lambda_init):
    b, s, _ = q.shape
    h = N_HEADS_A
    q = rms_norm(q.reshape(b, s, h, 2, HEAD_DIM), q_norm).transpose(0, 2, 3, 1, 4)
    k = rms_norm(k.reshape(b, s, h, 2, HEAD_DIM), k_norm).transpose(0, 2, 3, 1, 4)
    v = split_heads(v, h)
    lam = lam.astype(jnp.float32)
    lam_full = jnp.exp(jnp.sum(lam[0] * lam[1])) - jnp.exp(jnp.sum(lam[2] * lam[3])) + lambda_init
    slopes = alibi_slopes(h)
    scale = HEAD_DIM ** -0.5
    nb = s // Q_BLOCK
    kpos = jnp.arange(s)
    qb = q.reshape(b, h, 2, nb, Q_BLOCK, HEAD_DIM).transpose(3, 0, 1, 2, 4, 5)

    def block(args):
        qblk, i = args
        qpos = i * Q_BLOCK + jnp.arange(Q_BLOCK)
        dist = (qpos[:, None] - kpos[None, :]).astype(jnp.float32)
        bias = jnp.where(dist >= 0, -slopes[:, None, None] * dist, NEG_INF)
        sc = jnp.einsum('bhmqd,bhmkd->bhmqk', qblk, k).astype(jnp.float32) * scale + bias[None, :, None]
        p = jax.nn.softmax(sc, axis=-1)
        attn = p[:, :, 0] - lam_full * p[:, :, 1]
        return jnp.einsum('bhqk,bhkd->bhqd', attn.astype(v.dtype), v)

    o = unblock(lax.map(block, (qb, jnp.arange(nb))))
    o = rms_norm(o, subln) * (1.0 - lambda_init)
    return merge_heads(o)

def dilated_attention(q, k, v, q_norm, k_norm):
    b, s, _ = q.shape
    h = N_HEADS_B
    q = rms_norm(split_heads(q, h), q_norm)
    k = rms_norm(split_heads(k, h), k_norm)
    v = split_heads(v, h)
    slopes = alibi_slopes(h)
    scale = HEAD_DIM ** -0.5
    nb = s // Q_BLOCK
    qb = q.reshape(b, h, nb, Q_BLOCK, HEAD_DIM).transpose(2, 0, 1, 3, 4)

    def block(args):
        qblk, i = args
        qpos = i * Q_BLOCK + jnp.arange(Q_BLOCK)
        maxes, denoms, outs = [], [], []
        for window, dilation in DIL_PAIRS:
            offs = jnp.arange(window // dilation + 1) * dilation
            kidx = qpos[:, None] - offs[None, :]
            valid = kidx >= 0
            kidx = jnp.maximum(kidx, 0)
            kg = jnp.take(k, kidx, axis=2)
            vg = jnp.take(v, kidx, axis=2)
            sc = jnp.einsum('bhqd,bhqwd->bhqw', qblk, kg).astype(jnp.float32) * scale
            sc = sc - slopes[:, None, None] * offs.astype(jnp.float32)
            sc = jnp.where(valid, sc, NEG_INF)
            m = jnp.max(sc, axis=-1, keepdims=True)
            e = jnp.exp(sc - m)
            l = jnp.sum(e, axis=-1, keepdims=True)
            outs.append(jnp.einsum('bhqw,bhqwd->bhqd', (e / l).astype(v.dtype), vg).astype(jnp.float32))
            maxes.append(m)
            denoms.append(l)
        m_all = jnp.stack(maxes)
        wts = jnp.stack(denoms) * jnp.exp(m_all - jnp.max(m_all, axis=0))
        o = jnp.sum(wts * jnp.stack(outs), axis=0) / jnp.sum(wts, axis=0)
        return o.astype(v.dtype)

    return merge_heads(unblock(lax.map(block, (qb, jnp.arange(nb)))))

def moba_attention(q, k, v, q_norm, k_norm):
    b, s, _ = q.shape
    h = N_HEADS_C
    q = rms_norm(split_heads(q, h), q_norm)
    k = rms_norm(split_heads(k, h), k_norm)
    v = split_heads(v, h)
    nkb = -(-s // MOBA_BLOCK)
    pad = nkb * MOBA_BLOCK - s
    k_blk = jnp.pad(k, ((0, 0), (0, 0), (0, pad), (0, 0))).reshape(b, h, nkb, MOBA_BLOCK, HEAD_DIM)
    v_blk = jnp.pad(v, ((0, 0), (0, 0), (0, pad), (0, 0))).reshape(b, h, nkb, MOBA_BLOCK, HEAD_DIM)
    k_mean = jnp.mean(k_blk.astype(jnp.float32), axis=3)
    n_sel = min(MOBA_TOPK, nkb)
    n_keys = n_sel * MOBA_BLOCK
    slopes = alibi_slopes(h)
    scale = HEAD_DIM ** -0.5
    nc = s // MOBA_CHUNK
    qc = q.reshape(b, h, nc, MOBA_CHUNK, HEAD_DIM).transpose(2, 0, 1, 3, 4)
    offs = jnp.arange(MOBA_BLOCK)
    blk_ids = jnp.arange(nkb)
    bi = jnp.arange(b)[:, None, None, None]
    hi = jnp.arange(h)[None, :, None, None]

    def chunk(args):
        qblk, i = args
        qpos = i * MOBA_CHUNK + jnp.arange(MOBA_CHUNK)
        own = (i * MOBA_CHUNK) // MOBA_BLOCK
        gate = jnp.einsum('bhqd,bhnd->bhqn', qblk.astype(jnp.float32), k_mean)
        gate = jnp.where(blk_ids < own, gate, NEG_INF)
        _, sel = lax.top_k(gate, n_sel)
        sel_valid = jnp.repeat(jnp.arange(n_sel) < own, MOBA_BLOCK)
        kg = k_blk[bi, hi, sel].reshape(b, h, MOBA_CHUNK, n_keys, HEAD_DIM)
        vg = v_blk[bi, hi, sel].reshape(b, h, MOBA_CHUNK, n_keys, HEAD_DIM)
        kpos_sel = (sel[..., None] * MOBA_BLOCK + offs).reshape(b, h, MOBA_CHUNK, n_keys)
        dist_sel = (qpos[:, None] - kpos_sel).astype(jnp.float32)
        sc_sel = jnp.einsum('bhqd,bhqnd->bhqn', qblk, kg).astype(jnp.float32) * scale - slopes[:, None, None] * dist_sel
        sc_sel = jnp.where(sel_valid, sc_sel, NEG_INF)
        k_own = lax.dynamic_index_in_dim(k_blk, own, axis=2, keepdims=False)
        v_own = lax.dynamic_index_in_dim(v_blk, own, axis=2, keepdims=False)
        dist_own = (qpos[:, None] - (own * MOBA_BLOCK + offs)[None, :]).astype(jnp.float32)
        sc_own = jnp.einsum('bhqd,bhkd->bhqk', qblk, k_own).astype(jnp.float32) * scale - slopes[:, None, None] * dist_own
        sc_own = jnp.where(dist_own >= 0, sc_own, NEG_INF)
        p = jax.nn.softmax(jnp.concatenate([sc_sel, sc_own], axis=-1), axis=-1).astype(v.dtype)
        return (jnp.einsum('bhqn,bhqnd->bhqd', p[..., :n_keys], vg)
                + jnp.einsum('bhqk,bhkd->bhqd', p[..., n_keys:], v_own))

    return merge_heads(unblock(lax.map(chunk, (qc, jnp.arange(nc)))))

def stick_breaking_attention(q, k, v):
    b, s, _ = q.shape
    h = N_HEADS_D
    q = split_heads(q, h)
    k = split_heads(k, h)
    v = split_heads(v, h)
    scale = HEAD_DIM ** -0.5
    nb = s // Q_BLOCK
    kpos = jnp.arange(s)
    qb = q.reshape(b, h, nb, Q_BLOCK, HEAD_DIM).transpose(2, 0, 1, 3, 4)

    def block(args):
        qblk, i = args
        qpos = i * Q_BLOCK + jnp.arange(Q_BLOCK)
        strict = kpos[None, :] < qpos[:, None]
        z = jnp.einsum('bhqd,bhkd->bhqk', qblk, k).astype(jnp.float32) * scale
        log_keep = jnp.where(strict, jax.nn.log_sigmoid(-z), 0.0)
        log_a = jax.nn.log_sigmoid(z) + lax.cumsum(log_keep, axis=3, reverse=True) - log_keep
        a = jnp.where(strict, jnp.exp(log_a), 0.0)
        return jnp.einsum('bhqk,bhkd->bhqd', a.astype(v.dtype), v)

    return merge_heads(unblock(lax.map(block, (qb, jnp.arange(nb)))))

def setup_inputs(seed: int = 0) -> dict:
    key = jax.random.key(seed)
    ks = jax.random.split(key, 15)
    f32 = jnp.float32

    def nrm(k, shape, sd):
        return jax.random.normal(k, shape, f32) * sd

    return {
        'x': nrm(ks[0], (BATCH, SEQ, D_MODEL), 1.0),
        'c': nrm(ks[1], (BATCH, D_MODEL), 1.0),
        'norm_w': 1.0 + nrm(ks[2], (DEPTH, D_MODEL), 0.02),
        'w_mod': nrm(ks[3], (DEPTH, D_MODEL, 3 * D_MODEL), 0.5 * D_MODEL ** -0.5),
        'b_mod': nrm(ks[4], (DEPTH, 3 * D_MODEL), 0.02),
        'w_in': nrm(ks[5], (DEPTH, D_MODEL, IN_WIDTH), D_MODEL ** -0.5),
        'w_out': nrm(ks[6], (DEPTH, MIX_WIDTH, D_MODEL), MIX_WIDTH ** -0.5),
        'a_q_norm': 1.0 + nrm(ks[7], (N_EVEN, HEAD_DIM), 0.02),
        'a_k_norm': 1.0 + nrm(ks[8], (N_EVEN, HEAD_DIM), 0.02),
        'a_lambda': nrm(ks[9], (N_EVEN, 4, HEAD_DIM), 0.1),
        'a_subln': 1.0 + nrm(ks[10], (N_EVEN, 2 * HEAD_DIM), 0.02),
        'b_q_norm': 1.0 + nrm(ks[11], (N_EVEN, HEAD_DIM), 0.02),
        'b_k_norm': 1.0 + nrm(ks[12], (N_EVEN, HEAD_DIM), 0.02),
        'c_q_norm': 1.0 + nrm(ks[13], (N_ODD, HEAD_DIM), 0.02),
        'c_k_norm': 1.0 + nrm(ks[14], (N_ODD, HEAD_DIM), 0.02),
    }

def reference(x, c, norm_w, w_mod, b_mod, w_in, w_out, a_q_norm, a_k_norm, a_lambda, a_subln,
              b_q_norm, b_k_norm, c_q_norm, c_k_norm):
    c_act = jax.nn.silu(c)
    for layer in range(DEPTH):
        mod = c_act @ w_mod[layer] + b_mod[layer]
        shift, scale, gate = jnp.split(mod, 3, axis=-1)
        hdn = rms_norm(x, norm_w[layer]) * (1.0 + scale[:, None, :]) + shift[:, None, :]
        q1, k1, v1, g1, q2, k2, v2, g2 = jnp.split(hdn @ w_in[layer], 8, axis=-1)
        j = layer // 2
        if layer % 2 == 0:
            lambda_init = 0.8 - 0.6 * math.exp(-0.3 * layer)
            y1 = diff_attention(q1, k1, v1, a_q_norm[j], a_k_norm[j], a_lambda[j], a_subln[j], lambda_init)
            y2 = dilated_attention(q2, k2, v2, b_q_norm[j], b_k_norm[j])
        else:
            y1 = moba_attention(q1, k1, v1, c_q_norm[j], c_k_norm[j])
            y2 = stick_breaking_attention(q2, k2, v2)
        y = jnp.concatenate([y1 * jax.nn.silu(g1), y2 * jax.nn.silu(g2)], axis=-1) @ w_out[layer]
        x = x + gate[:, None, :] * y
    return x


_drawn_inputs = setup_inputs


def setup_inputs(seed=0):
    import zlib

    import numpy as np

    out = dict(_drawn_inputs(seed))
    spreads = {}
    factors = {'norm_w': 8.0,
     'b_mod': 3.503,
     'a_q_norm': 8.0,
     'a_k_norm': 8.0,
     'a_lambda': 8.0,
     'a_subln': 8.0,
     'b_q_norm': 8.0,
     'b_k_norm': 8.0,
     'c_q_norm': 8.0,
     'c_k_norm': 8.0}
    for name, (base, spread) in spreads.items():
        noise = np.random.default_rng([zlib.crc32(name.encode()), seed]).standard_normal(out[name].shape)
        drawn = base * np.exp(spread * noise) if base else spread * noise
        out[name] = __import__('jax').numpy.asarray(drawn.astype(out[name].dtype))
    for name, factor in factors.items():
        out[name] = (out[name] * factor).astype(out[name].dtype)
    return out
```

```python
import math
from contextlib import ExitStack

import concourse.bass as bass
from concourse import mybir

F32 = mybir.dt.float32
F32R = mybir.dt.float32r
BF16 = mybir.dt.bfloat16
ALU = mybir.AluOpType
ACT = mybir.ActivationFunctionType
AX = mybir.AxisListType

P = 128
D = 1024
S = 256
LAYERS = 2
KB = D // P
HD = 64
EPS = 1e-6
SCALE = HD ** -0.5
MASKED = 1e30
LAMBDA_INIT = 0.8 - 0.6 * math.exp(-0.3 * 0)
CHUNK = 512
UNIT = 256
RAW = 3
MAPW = 384

IN_UNITS = 16
UNITS = 20
SLOTS = 2 * UNITS
ORDER = (1, 0, 2, 5, 4, 6, 3, 7)
K1, Q1, V1, K2, Q2, V2, G1, G2 = range(8)
FIRST_MAP = (11, 23)
FIRST_D = 21
TRI_LAG, PV_LAG_D = 2, 3
GATE_AT = (28, 30, 31, 32)
SUBLN_AT = (24, 26)

MOD_GROUPS = ((1, 9), (2, 33))

R_C, R_NORM, R_BMOD = 0, KB, KB + LAYERS * KB
R_QK = R_BMOD + LAYERS * 3 * KB
R_SUBLN = R_QK + 6
ROWS = R_SUBLN + 1

C_DIST, C_CAUSAL, C_DIL = 0, 256, 512
C_ID, C_HEAD, C_MEAN128, C_MEAN, C_TRI, C_NEG = (768 + P * i for i in range(6))
CONSTS = 768 + P * 6

V_A, V_B, V_GATE = 0, 2 * KB, 4 * KB
V_QK = 6 * KB
V_SUBLN = V_QK + 6
V_CACT = V_SUBLN + 1
V_TMP = V_CACT + KB
V_LAM = V_TMP + 8
V_EPS = V_LAM + 8
V_N = V_EPS + 2


def maps_at(layer, h, lag=0):
    h -= lag
    out = [h - FIRST_MAP[0]] if 0 <= h - FIRST_MAP[0] < 8 else []
    if layer == 0 and 0 <= h - FIRST_MAP[1] < 8:
        out.append(8 + h - FIRST_MAP[1])
    return out


def sticks_at(layer, h, lag=0):
    h -= lag
    return [h - FIRST_D] if layer == 1 and 0 <= h - FIRST_D < 8 else []


def head_of(layer, m):
    if layer == 0 and m < 8:
        return m // 2 if m % 2 else None
    return m - 4 if layer == 0 else 12 + m


def normed(layer, u):
    return u < IN_UNITS and u // 2 in ((K1, Q1, K2, Q2) if layer == 0 else (K1, Q1))


def norms():
    out = []
    for layer in range(LAYERS):
        out.append((layer, -1, "rms", 0))
        for h in range(SLOTS):
            if h % 2 and h >= 3 and normed(layer, (h - 3) // 2):
                out.append((layer, h, "unit", (h - 3) // 2))
            if layer == 0 and h in SUBLN_AT:
                out.append((layer, h, "subln", SUBLN_AT.index(h)))
    return out


NORMS = norms()


def norm_at(layer, h):
    return [(j, kind, i) for j, (la, hh, kind, i) in enumerate(NORMS) if (la, hh) == (layer, h)]


def freed_by_vector(n):
    u = n % UNITS
    return u // 2 in (G1, G2) or u >= IN_UNITS


def frees(n, vector):
    return sum(freed_by_vector(i) == vector for i in range(n + 1))


SQUARED = [sum(kind != "rms" for _, _, kind, _ in NORMS[:j + 1]) for j in range(len(NORMS))]
UNIT_NORMS = [j for j, (_, _, kind, _) in enumerate(NORMS) if kind == "unit"]


def turned_by(layer, m):
    return m // 2 + 1 if layer == 0 and m < 8 else (m - 3 if layer == 0 else 13 + m)


def slope(layer, m):
    if layer == 0 and m < 8:
        return 2.0 ** (-8.0 * (m // 2 + 1) / 4)
    return 2.0 ** (-(m % 8 + 1))


def program(nc, x, c, norm_w, w_mod, b_mod, w_in, w_out, a_q_norm, a_k_norm, a_lambda, a_subln,
            b_q_norm, b_k_norm, c_q_norm, c_k_norm, consts, out):
    with ExitStack() as ctx:
        def sb(name, shape, dt=F32):
            return ctx.enter_context(nc.sbuf_tensor(name, shape, dt))

        def bank(name):
            return ctx.enter_context(nc.psum_tensor(name, [P, 512], F32))

        def sem(name):
            return ctx.enter_context(nc.semaphore(name))

        raw = sb("raw", [P, RAW, KB, CHUNK])
        w_hi = sb("w_hi", [P, 2, KB, UNIT], F32R)
        w_lo = sb("w_lo", [P, 2, KB, UNIT], F32R)
        h_hi = sb("h_hi", [P, KB, S], F32R)
        h_lo = sb("h_lo", [P, KB, S], F32R)
        y_hi = sb("y_hi", [P, KB, S], F32R)
        y_lo = sb("y_lo", [P, KB, S], F32R)
        xT = sb("xT", [P, KB, S])
        y = sb("y", [P, KB, S])
        gates = sb("gates", [P, KB, S])
        kT = sb("kT", [P, 2, 4, S])
        qZ = sb("qZ", [P, 2, 8, S])
        val = sb("val", [P, 2, 2, CHUNK])
        n_raw = sb("n_raw", [P, 2, 512])
        n_sq = sb("n_sq", [P, 512])
        n_y0 = sb("n_y0", [P, 512])
        n_t = sb("n_t", [P, 512])
        logits = sb("logits", [P, 2, 512])
        probs = sb("probs", [P, 3, 512])
        probsT = sb("probsT", [P, 2, 512])
        bias = sb("bias", [P, 2, S])
        acc_v = sb("acc_v", [P, CHUNK])
        acc_g = sb("acc_g", [P, CHUNK])
        rows = sb("rows", [P, P])
        cols = sb("cols", [P, ROWS])
        v = sb("v", [P, V_N])
        lam = sb("lam", [P, 4, HD])
        cst = sb("cst", [P, CONSTS])
        mask_id = sb("mask_id", [P, P], BF16)
        mask_tri = sb("mask_tri", [P, P], BF16)
        stat = sb("stat", [P, 2, 8])

        dist, causal, dilated = (cst[:, o:o + S] for o in (C_DIST, C_CAUSAL, C_DIL))
        ident, head_mean, mean128, mean, tri, neg = (
            cst[:, o:o + P] for o in (C_ID, C_HEAD, C_MEAN128, C_MEAN, C_TRI, C_NEG))
        x_tok = y[:, :, :].rearrange("p a b -> p (a b)").rearrange("p (t f) -> p t f", t=2)
        out_tok = x_tok

        proj = [bank("proj0"), bank("proj1")]
        sumsq = bank("sumsq")
        score = [bank("score0"), bank("score1"), bank("turned")]
        turned = score[2]
        mixed = bank("mixed")
        final = score + [mixed]
        small = bank("small")

        raw_full = [sem(f"raw_full{i}") for i in range(RAW)]
        x_in, vec_in, cst_in, lam_in = sem("x_in"), sem("vec_in"), sem("cst_in"), sem("lam_in")
        masks_ok = sem("masks_ok")
        padded = sem("padded")
        zeroed = sem("zeroed")
        cols_T, cols_ok = sem("cols_T"), sem("cols_ok")
        act_c = sem("act_c")
        vec_c = sem("vec_c")
        xT_T, xT_ok = sem("xT_T"), sem("xT_ok")
        mod_v = sem("mod_v")
        mod_T, mod_ok = sem("mod_T"), sem("mod_ok")
        hi_done, lo_done = sem("hi_done"), sem("lo_done")
        xsq = sem("xsq")
        h_pre, h_hi_ok, h_ok = sem("h_pre"), sem("h_hi_ok"), sem("h_ok")
        proj_done = sem("proj_done")
        free_act, free_dve = sem("free_act"), sem("free_dve")
        sq_ok, ssq_ok = sem("sq_ok"), sem("ssq_ok")
        ln_ok, y0_ok = sem("ln_ok"), sem("y0_ok")
        nt_ok, norm_ok = sem("nt_ok"), sem("norm_ok")
        e_gate, gate_ok = sem("e_gate"), sem("gate_ok")
        slope_ok, bias_ok = sem("slope_ok"), sem("bias_ok")
        score_ok, logit_ok, exp_ok, prob_ok = (sem(n) for n in ("score_ok", "logit_ok", "exp_ok", "prob_ok"))
        turn_ok, probsT_ok, pv_ok, y_raw = (sem(n) for n in ("turn_ok", "probsT_ok", "pv_ok", "y_raw"))
        d_abs, d_exp, d_ln, d_sp = (sem(n) for n in ("d_abs", "d_exp", "d_ln", "d_sp"))
        d_tri, d_a = sem("d_tri"), sem("d_a")
        y_ok, y_hi_ok, y_lo_ok = sem("y_ok"), sem("y_hi_ok"), sem("y_lo_ok")
        out_T, out_ok, stored = sem("out_T"), sem("out_ok"), sem("stored")
        pool_step = sem("pool_step")
        dve_step = sem("dve_step")

        chunks = [("mod_v", i) for i in range(4)]
        for i in range(8):
            chunks += [("w", i), ("mod_g", i)]
        chunks += [("w", i) for i in range(8, UNITS)]
        place = {key: n for n, key in enumerate(chunks)}

        def source(kind, i):
            if kind == "mod_v":
                w, col = w_mod[0], CHUNK * i
            elif kind == "mod_g":
                w, col = (w_mod[0], CHUNK * (4 + i)) if i < 2 else (w_mod[1], CHUNK * (i - 2))
            elif i % 10 < 8:
                w, col = w_in[i // 10], CHUNK * ORDER[i % 10]
            else:
                w, col = w_out[i // 10], CHUNK * (i % 10 - 8)
            return w[:, col:col + CHUNK].rearrange("(k p) n -> p k n", p=P)

        def wait_raw(eng, key):
            n = place[key]
            eng.wait_ge(raw_full[n % RAW], 16 * (n // RAW + 1))

        block = ctx.enter_context(nc.Block())

        @block.sync
        def _(sp):
            def load(n):
                kind, i = chunks[n]
                if n >= RAW:
                    was, j = chunks[n - RAW]
                    if was == "mod_v":
                        sp.wait_ge(mod_v, j + 1)
                    elif was == "mod_g":
                        sp.wait_ge(pool_step, 2 * KB * (j + 1))
                    else:
                        sp.wait_ge(lo_done, 4 * (j + 1))
                sp.dma_start(raw[:, n % RAW, :, :], source(kind, i)).then_inc(raw_full[n % RAW], 16)

            for n in range(len(chunks)):
                load(n)
            for i in range(4):
                t, half = i % 2, i // 2
                sp.wait_ge(out_ok, i + 1)
                sp.dma_start(out[0, t * P:(t + 1) * P, half * 512:(half + 1) * 512],
                             out_tok[:, t, half * 512:(half + 1) * 512]).then_inc(stored, 16)
            sp.wait_ge(stored, 64)

        @block.scalar
        def _(act):
            act.dma_start(x_tok, x[0].rearrange("(t p) f -> p t f", p=P)).then_inc(x_in, 16)
            act.dma_start(cst[:, :], consts).then_inc(cst_in, 16)
            act.wait_ge(padded, 1)
            act.dma_start(rows[R_C:R_C + KB, :], c.rearrange("b (k p) -> (b k) p", p=P)).then_inc(vec_in, 16)
            act.dma_start(rows[R_NORM:R_BMOD, :], norm_w.rearrange("l (k p) -> (l k) p", p=P)).then_inc(vec_in, 16)
            act.dma_start(rows[R_BMOD:R_QK, :], b_mod.rearrange("l (k p) -> (l k) p", p=P)).then_inc(vec_in, 16)
            for i, w in enumerate((a_q_norm, a_k_norm, b_q_norm, b_k_norm, c_q_norm, c_k_norm)):
                for side in range(2):
                    act.dma_start(rows[R_QK + i:R_QK + i + 1, side * HD:(side + 1) * HD], w).then_inc(vec_in, 16)
            act.dma_start(rows[R_SUBLN:R_SUBLN + 1, :], a_subln).then_inc(vec_in, 16)
            act.dma_start(lam[:, :, :], a_lambda.rearrange("a i d -> a (i d)").broadcast_to([P, 4 * HD])
                          .rearrange("p (i d) -> p i d", i=4)).then_inc(lam_in, 16)

            for i in range(4):
                act.wait_ge(xT_T, i + 1)
                nc.scalar.activation(xT[:, 2 * i:2 * i + 2, :], proj[i % 2][:, :], ACT.Copy).then_inc(xT_ok, 1)
            act.wait_ge(cols_ok, 1)
            nc.scalar.activation(v[:, V_CACT:V_CACT + KB], cols[:, R_C:R_C + KB], ACT.Exp, scale=-1.0).then_inc(act_c, 1)
            act.wait_ge(vec_c, 1)
            nc.scalar.activation(v[:, V_LAM + 2:V_LAM + 4], v[:, V_LAM:V_LAM + 2], ACT.Exp).then_inc(act_c, 1)

            def split_hi(n, half):
                ks = slice(4 * half, 4 * half + 4)
                wait_raw(act, ("w", n // 2))
                if n >= 2:
                    act.wait_ge(proj_done, n - 1)
                nc.scalar.activation(w_hi[:, n % 2, ks, :],
                                     raw[:, place["w", n // 2] % RAW, ks, (n % 2) * UNIT:(n % 2 + 1) * UNIT],
                                     ACT.Copy).then_inc(hi_done, 1)

            def norm_seed(j, width):
                act.wait_ge(ssq_ok, j + 1)
                if j:
                    act.wait_ge(norm_ok, j)
                nc.scalar.activation(n_y0[:, 0:width], sumsq[:, 0:width], ACT.Ln,
                                     bias=v[:, V_EPS:V_EPS + 1]).then_inc(ln_ok, 1)
                act.wait_ge(ln_ok, j + 1)
                nc.scalar.activation(n_y0[:, 0:width], n_y0[:, 0:width], ACT.Exp, scale=-0.5).then_inc(y0_ok, 1)

            def take_unit(layer, u):
                n = UNITS * layer + u
                group, part = u // 2, u % 2
                b = proj[n % 2]
                act.wait_ge(proj_done, n + 1)
                if normed(layer, u):
                    r = UNIT_NORMS.index(norm_of[layer, u])
                    if r >= 2:
                        act.wait_ge(norm_ok, UNIT_NORMS[r - 2] + 1)
                    nc.scalar.activation(n_raw[:, r % 2, :], b[:, :], ACT.Copy).then_inc(free_act, 1)
                elif group in (V1, V2):
                    nc.scalar.activation(val[:, int(group == V2), :, part * UNIT:(part + 1) * UNIT],
                                         b[:, :].rearrange("p (t n) -> p t n", t=2), ACT.Copy).then_inc(free_act, 1)
                elif group == K2:
                    nc.scalar.activation(kT[:, 1, 2 * part:2 * part + 2, :],
                                         b[:, :].rearrange("p (a s) -> p a s", a=2), ACT.Copy).then_inc(free_act, 1)
                elif group == Q2:
                    act.wait_ge(zeroed, 4)
                    for odd in range(2):
                        half = slice(HD * odd, HD * odd + HD)
                        i = nc.scalar.activation(qZ[half, 1, 4 * part + odd:4 * part + 4:2, :],
                                                 b[half, :].rearrange("p (a s) -> p a s", a=2), ACT.Copy, scale=SCALE)
                    i.then_inc(free_act, 1)
                else:
                    i = 2 * (group - G1) + part
                    act.wait_ge(h_ok, KB * (layer + 1))
                    nc.scalar.activation(gates[:, 2 * i:2 * i + 2, :],
                                         b[:, :].rearrange("p (a s) -> p a s", a=2), ACT.Exp, scale=-1.0).then_inc(e_gate, 1)

            norm_of = {(la, i): j for j, (la, _, kind, i) in enumerate(NORMS) if kind == "unit"}

            split_hi(0, 0)
            split_hi(0, 1)
            for layer in range(LAYERS):
                for i in range(4):
                    if layer:
                        act.wait_ge(free_dve, frees(UNITS * layer - 4 + i, True))
                        act.wait_ge(y_ok, 4 * layer)
                    else:
                        act.wait_ge(xT_ok, i + 1)
                    nc.scalar.activation(gates[:, 2 * i:2 * i + 2, :], xT[:, 2 * i:2 * i + 2, :], ACT.Square).then_inc(xsq, 1)
                norm_seed(norm_at(layer, -1)[0][0], S)
                for k in range(KB):
                    act.wait_ge(h_pre, KB * layer + k + 1)
                    nc.scalar.activation(h_hi[:, k, :], gates[:, k, :], ACT.Identity,
                                         bias=v[:, V_B + KB * layer + k:V_B + KB * layer + k + 1]).then_inc(h_hi_ok, 1)
                for h in range(SLOTS):
                    n = UNITS * layer + h // 2
                    if h % 2 and h < 2 * IN_UNITS:
                        take_unit(layer, h // 2)
                    for j, _, _ in norm_at(layer, h):
                        norm_seed(j, 512)
                    for m in maps_at(layer, h, 1):
                        t = head_of(layer, m)
                        if t is not None:
                            act.wait_ge(turn_ok, t + 1)
                            if t >= 2:
                                act.wait_ge(pv_ok, t - 1)
                            nc.scalar.activation(probsT[:, t % 2, 0:MAPW], turned[:, 0:MAPW], ACT.Copy).then_inc(probsT_ok, 1)
                    for m in maps_at(layer, h, 2):
                        t = head_of(layer, m)
                        if t is not None and (layer == 0 and m < 8 or m % 2):
                            blk = m // 2
                            act.wait_ge(pv_ok, t + 1)
                            nc.scalar.activation(y[:, blk, :], mixed[:, 0:S], ACT.Copy).then_inc(y_raw, 1)
                    for m in sticks_at(layer, h, TRI_LAG):
                        act.wait_ge(d_tri, m + 1)
                        act.wait_ge(pv_ok, 20 + m - 1)
                        nc.scalar.activation(probsT[:, m % 2, 0:MAPW], score[m % 3][:, 0:MAPW], ACT.Exp).then_inc(d_a, 1)
                    for m in sticks_at(layer, h, PV_LAG_D):
                        if m % 2:
                            act.wait_ge(pv_ok, 20 + m + 1)
                            nc.scalar.activation(y[:, 4 + m // 2, :], mixed[:, 0:S], ACT.Copy).then_inc(y_raw, 1)
                    for m in maps_at(layer, h):
                        M = 16 * layer + m
                        act.wait_ge(logit_ok, M + 1)
                        if M >= 2:
                            act.wait_ge(prob_ok, M - 1)
                        if M >= 3:
                            act.wait_ge(turn_ok, turned_by((M - 3) // 16, (M - 3) % 16))
                        for tile, cs in enumerate((slice(0, P), slice(P, MAPW))):
                            i = nc.scalar.activation(probs[:, M % 3, cs], logits[:, M % 2, cs], ACT.Exp, scale=-1.0,
                                                     bias=stat[:, M % 2, tile:tile + 1],
                                                     accum_out=stat[:, M % 2, 2 + tile:3 + tile])
                        i.then_inc(exp_ok, 1)
                    for m in sticks_at(layer, h):
                        act.wait_ge(score_ok, 24 + m + 1)
                        act.wait_ge(d_sp, m - 1) if m >= 2 else act.wait_ge(prob_ok, 24)
                        nc.scalar.activation(logits[:, m % 2, 0:MAPW], score[m % 3][:, 0:MAPW], ACT.Abs).then_inc(d_abs, 1)
                        act.wait_ge(d_abs, m + 1)
                        nc.scalar.activation(logits[:, m % 2, 0:MAPW], logits[:, m % 2, 0:MAPW], ACT.Exp, scale=-1.0).then_inc(d_exp, 1)
                        act.wait_ge(d_exp, m + 1)
                        nc.scalar.activation(logits[:, m % 2, 0:MAPW], logits[:, m % 2, 0:MAPW], ACT.Ln, bias=1.0).then_inc(d_ln, 1)
                    if h in GATE_AT:
                        i = GATE_AT.index(h)
                        act.wait_ge(y_ok, 4 * layer + i + 1)
                        nc.scalar.activation(y_hi[:, 2 * i:2 * i + 2, :], y[:, 2 * i:2 * i + 2, :], ACT.Copy).then_inc(y_hi_ok, 1)
                    if n + 1 < UNITS * LAYERS:
                        split_hi(n + 1, h % 2)
            for i in range(4):
                act.wait_ge(out_T, i + 1)
                nc.scalar.activation(out_tok[:, i % 2, (i // 2) * 512:(i // 2 + 1) * 512],
                                     final[i][:, :], ACT.Copy).then_inc(out_ok, 1)

        @block.vector
        def _(dve):
            steps = [0]

            def link(ins):
                steps[0] += 1
                ins.then_inc(dve_step, 1)
                dve.wait_ge(dve_step, steps[0])

            def col(i, n=1):
                return v[:, i:i + n]

            nc.vector.memset(rows[:, :], 0.0).then_inc(padded, 1)
            nc.vector.memset(col(V_EPS), EPS)
            nc.vector.memset(col(V_EPS + 1), 1.0)

            dve.wait_ge(cst_in, 16)
            nc.vector.tensor_scalar_mul(mask_id[:, :], ident, MASKED)
            nc.vector.tensor_copy(mask_tri[:, :], tri).then_inc(masks_ok, 1)
            dve.wait_ge(cols_T, 1)
            nc.vector.tensor_copy(cols[:, :], small[:, P:P + ROWS]).then_inc(cols_ok, 1)
            dve.wait_ge(lam_in, 16)
            for i in range(2):
                j = nc.vector.tensor_tensor_reduce(out=n_t[:, 0:HD], in0=lam[:, 2 * i, :], in1=lam[:, 2 * i + 1, :],
                                                   scale=1.0, scalar=0.0, op0=ALU.mult, op1=ALU.add,
                                                   accum_out=col(V_LAM + i))
                if i == 0:
                    link(j)
            j.then_inc(vec_c, 1)
            dve.wait_ge(act_c, 1)
            dve.wait_ge(cols_ok, 1)
            link(nc.vector.tensor_scalar_add(col(V_CACT, KB), col(V_CACT, KB), 1.0))
            link(nc.vector.reciprocal(col(V_CACT, KB), col(V_CACT, KB)))
            nc.vector.tensor_tensor(col(V_CACT, KB), col(V_CACT, KB), cols[:, R_C:R_C + KB], ALU.mult).then_inc(vec_c, 1)
            dve.wait_ge(act_c, 2)
            nc.vector.scalar_tensor_tensor(out=col(V_LAM + 4), in0=col(V_LAM + 3), scalar=-LAMBDA_INIT,
                                           in1=col(V_LAM + 2), op0=ALU.add, op1=ALU.subtract)
            for i in range(6):
                f = 0.5 * SCALE if i % 2 == 0 else -0.5
                nc.vector.tensor_scalar_mul(col(V_QK + i), cols[:, R_QK + i:R_QK + i + 1], f)
            link(nc.vector.tensor_scalar_mul(col(V_SUBLN), cols[:, R_SUBLN:R_SUBLN + 1], -0.5 * (1.0 - LAMBDA_INIT)))

            dve.wait_ge(vec_c, 2)
            for i in range(4):
                wait_raw(dve, ("mod_v", i))
                if i:
                    dve.wait_ge(mod_T, i)
                w = raw[:, place["mod_v", i] % RAW, :, :]
                link(nc.vector.tensor_scalar_mul(acc_v[:, :], w[:, 0, :], col(V_CACT)))
                for k in range(1, KB):
                    j = nc.vector.scalar_tensor_tensor(out=acc_v[:, :], in0=w[:, k, :], scalar=col(V_CACT + k),
                                                       in1=acc_v[:, :], op0=ALU.mult, op1=ALU.add)
                    if k < KB - 1:
                        link(j)
                j.then_inc(mod_v, 1)

            def take_shift_scale(layer):
                o = 32 * layer
                b = R_BMOD + 3 * KB * layer
                nw = R_NORM + KB * layer
                nc.vector.tensor_tensor(col(V_B + KB * layer, KB), small[:, o:o + KB], cols[:, b:b + KB], ALU.add)
                link(nc.vector.tensor_tensor(col(V_TMP, KB), small[:, o + KB:o + 2 * KB],
                                             cols[:, b + KB:b + 2 * KB], ALU.add))
                link(nc.vector.scalar_tensor_tensor(out=col(V_TMP, KB), in0=col(V_TMP, KB), scalar=1.0,
                                                    in1=cols[:, nw:nw + KB], op0=ALU.add, op1=ALU.mult))
                return nc.vector.tensor_scalar_mul(col(V_A + KB * layer, KB), col(V_TMP, KB), -0.5)

            def take_gate(layer):
                o = 32 * layer + 2 * KB
                b = R_BMOD + 3 * KB * layer + 2 * KB
                return nc.vector.tensor_tensor(col(V_GATE + KB * layer, KB), small[:, o:o + KB],
                                               cols[:, b:b + KB], ALU.add)

            dve.wait_ge(mod_T, 4)
            take_shift_scale(0).then_inc(mod_ok, 1)
            dve.wait_ge(mod_ok, 1)

            def split_lo(n, half):
                ks = slice(4 * half, 4 * half + 4)
                dve.wait_ge(hi_done, 2 * n + half + 1)
                nc.vector.tensor_tensor(w_lo[:, n % 2, ks, :],
                                        raw[:, place["w", n // 2] % RAW, ks, (n % 2) * UNIT:(n % 2 + 1) * UNIT],
                                        w_hi[:, n % 2, ks, :], ALU.subtract).then_inc(lo_done, 1)

            def refine(j, width):
                dve.wait_ge(y0_ok, j + 1)
                nc.vector.scalar_tensor_tensor(out=n_t[:, 0:width], in0=sumsq[:, 0:width], scalar=EPS,
                                               in1=n_y0[:, 0:width], op0=ALU.add, op1=ALU.mult).then_inc(nt_ok, 1)
                dve.wait_ge(nt_ok, j + 1)
                link(nc.vector.tensor_tensor(n_t[:, 0:width], n_t[:, 0:width], n_y0[:, 0:width], ALU.mult))
                link(nc.vector.scalar_tensor_tensor(out=n_t[:, 0:width], in0=n_t[:, 0:width], scalar=-3.0,
                                                    in1=n_y0[:, 0:width], op0=ALU.add, op1=ALU.mult))

            def norm_unit(j, layer, u):
                refine(j, 512)
                r = UNIT_NORMS.index(j)
                grp, part = u // 6, u % 2
                is_k = u // 2 in (K1, K2)
                w = V_QK + 4 * layer + 2 * grp + is_k
                if is_k:
                    i = nc.vector.scalar_tensor_tensor(
                        out=kT[:, grp, 2 * part:2 * part + 2, :],
                        in0=n_raw[:, r % 2, :].rearrange("p (a s) -> p a s", a=2), scalar=col(w),
                        in1=n_t[:, :].rearrange("p (a s) -> p a s", a=2), op0=ALU.mult, op1=ALU.mult)
                else:
                    dve.wait_ge(zeroed, 4)
                    for odd in range(2):
                        half = slice(HD * odd, HD * odd + HD)
                        i = nc.vector.scalar_tensor_tensor(
                            out=qZ[half, grp, 4 * part + odd:4 * part + 4:2, :],
                            in0=n_raw[half, r % 2, :].rearrange("p (a s) -> p a s", a=2), scalar=v[half, w:w + 1],
                            in1=n_t[half, :].rearrange("p (a s) -> p a s", a=2), op0=ALU.mult, op1=ALU.mult)
                i.then_inc(norm_ok, 1)

            def norm_subln(j, i):
                refine(j, 512)
                nc.vector.scalar_tensor_tensor(
                    out=y[:, 2 * i:2 * i + 2, :], in0=y[:, 2 * i:2 * i + 2, :], scalar=col(V_SUBLN),
                    in1=n_t[:, :].rearrange("p (a s) -> p a s", a=2), op0=ALU.mult, op1=ALU.mult).then_inc(norm_ok, 1)

            split_lo(0, 0)
            split_lo(0, 1)
            for layer in range(LAYERS):
                j = norm_at(layer, -1)[0][0]
                refine(j, S)
                for k in range(KB):
                    nc.vector.scalar_tensor_tensor(out=gates[:, k, :], in0=xT[:, k, :], scalar=col(V_A + KB * layer + k),
                                                   in1=n_t[:, 0:S], op0=ALU.mult, op1=ALU.mult).then_inc(h_pre, 1)
                for k in range(KB):
                    dve.wait_ge(h_hi_ok, KB * layer + k + 1)
                    nc.vector.scalar_tensor_tensor(out=h_lo[:, k, :], in0=gates[:, k, :], scalar=col(V_B + KB * layer + k),
                                                   in1=h_hi[:, k, :], op0=ALU.add, op1=ALU.subtract).then_inc(h_ok, 1)
                dve.wait_ge(h_ok, KB * (layer + 1))
                nc.vector.tensor_copy(col(V_TMP), col(V_EPS)).then_inc(norm_ok, 1)
                for h in range(SLOTS):
                    u = h // 2
                    n = UNITS * layer + u
                    for j, kind, i in norm_at(layer, h - 1) if h else []:
                        if kind == "unit":
                            norm_unit(j, layer, i)
                        else:
                            norm_subln(j, i)
                    if h % 2 and u < IN_UNITS and u // 2 in (G1, G2):
                        i = u - 2 * G1
                        g = gates[:, 2 * i:2 * i + 2, :]
                        dve.wait_ge(e_gate, 4 * layer + i + 1)
                        link(nc.vector.tensor_scalar_add(g, g, 1.0))
                        link(nc.vector.reciprocal(g, g))
                        nc.vector.tensor_tensor(g, proj[n % 2][:, :].rearrange("p (a s) -> p a s", a=2), g,
                                                ALU.mult).then_inc(free_dve, 1)
                        dve.wait_ge(free_dve, frees(n, True))
                    if h % 2 and u >= IN_UNITS:
                        i = u - IN_UNITS
                        dve.wait_ge(proj_done, n + 1)
                        for fb in range(2):
                            k = 2 * i + fb
                            s = nc.vector.scalar_tensor_tensor(
                                out=xT[:, k, :], in0=proj[n % 2][:, fb * S:(fb + 1) * S],
                                scalar=col(V_GATE + KB * layer + k), in1=xT[:, k, :], op0=ALU.mult, op1=ALU.add)
                        s.then_inc(free_dve, 1)
                    for m in maps_at(layer, h):
                        M = 16 * layer + m
                        dve.wait_ge(score_ok, M + 1)
                        dve.wait_ge(bias_ok, M + 1)
                        if M >= 2:
                            dve.wait_ge(exp_ok, M - 1)
                        for tile, (cs, bs) in enumerate(((slice(0, P), slice(P, S)), (slice(P, MAPW), slice(0, S)))):
                            i = nc.vector.tensor_tensor_reduce(
                                out=logits[:, M % 2, cs], in0=score[M % 2][:, cs], in1=bias[:, M % 2, bs],
                                scale=1.0, scalar=3e38, op0=ALU.add, op1=ALU.min,
                                accum_out=stat[:, M % 2, tile:tile + 1])
                        i.then_inc(logit_ok, 1)
                    if h in GATE_AT:
                        i = GATE_AT.index(h)
                        ys = y[:, 2 * i:2 * i + 2, :]
                        dve.wait_ge(y_raw, 8 * layer + 2 * i + 2)
                        nc.vector.tensor_tensor(ys, ys, gates[:, 2 * i:2 * i + 2, :], ALU.mult).then_inc(y_ok, 1)
                    if n + 1 < UNITS * LAYERS:
                        split_lo(n + 1, h % 2)
                    for m in maps_at(layer, h):
                        M = 16 * layer + m
                        dve.wait_ge(exp_ok, M + 1)
                        st = stat[:, M % 2, :]
                        link(nc.vector.reciprocal(st[:, 4:6], st[:, 2:4]))
                        for tile, cs in enumerate((slice(0, P), slice(P, MAPW))):
                            if layer == 0 and m < 8 and m % 2:
                                if tile == 0:
                                    link(nc.vector.tensor_scalar_mul(st[:, 6:8], st[:, 4:6], col(V_LAM + 4)))
                                i = nc.vector.scalar_tensor_tensor(
                                    out=probs[:, M % 3, cs], in0=probs[:, M % 3, cs], scalar=st[:, 6 + tile:7 + tile],
                                    in1=probs[:, (M - 1) % 3, cs], op0=ALU.mult, op1=ALU.add)
                            else:
                                i = nc.vector.tensor_scalar_mul(probs[:, M % 3, cs], probs[:, M % 3, cs],
                                                                st[:, 4 + tile:5 + tile])
                        i.then_inc(prob_ok, 1)
                        dve.wait_ge(prob_ok, M + 1)
                    for m in sticks_at(layer, h):
                        dve.wait_ge(d_ln, m + 1)
                        if m >= 3:
                            dve.wait_ge(d_tri, m - 2)
                        else:
                            dve.wait_ge(turn_ok, 20)
                        nc.vector.scalar_tensor_tensor(
                            out=probs[:, m % 3, 0:MAPW], in0=score[m % 3][:, 0:MAPW], scalar=0.0,
                            in1=logits[:, m % 2, 0:MAPW], op0=ALU.max, op1=ALU.add).then_inc(d_sp, 1)
                    if h in GATE_AT:
                        i = GATE_AT.index(h)
                        dve.wait_ge(y_hi_ok, 4 * layer + i + 1)
                        nc.vector.tensor_tensor(y_lo[:, 2 * i:2 * i + 2, :], y[:, 2 * i:2 * i + 2, :],
                                                y_hi[:, 2 * i:2 * i + 2, :], ALU.subtract).then_inc(y_lo_ok, 1)
                    if layer == 0 and h == MOD_GROUPS[0][1]:
                        dve.wait_ge(mod_T, 6)
                        take_gate(0).then_inc(mod_ok, 1)
                    if layer == 0 and h == MOD_GROUPS[1][1]:
                        dve.wait_ge(mod_T, 12)
                        take_shift_scale(1)
                        take_gate(1).then_inc(mod_ok, 1)
                        dve.wait_ge(mod_ok, 3)

        @block.gpsimd
        def _(pool):
            for grp in range(2):
                for odd in range(2):
                    nc.gpsimd.memset(qZ[HD * (1 - odd):HD * (2 - odd), grp, odd::2, :], 0.0).then_inc(zeroed, 1)
                    pool.wait_ge(zeroed, 2 * grp + odd + 1)
            pool.wait_ge(cst_in, 16)

            def square(layer, h):
                for j, kind, i in norm_at(layer, h):
                    pool.wait_ge(ssq_ok, j)
                    if kind == "unit":
                        r = UNIT_NORMS.index(j)
                        n = UNITS * layer + i
                        pool.wait_ge(free_act, frees(n, False))
                        nc.gpsimd.tensor_tensor(n_sq[:, :], n_raw[:, r % 2, :], n_raw[:, r % 2, :], ALU.mult).then_inc(sq_ok, 1)
                    else:
                        ys = y[:, 2 * i:2 * i + 2, :]
                        pool.wait_ge(y_raw, 2 * i + 2)
                        nc.gpsimd.tensor_tensor(n_sq[:, :].rearrange("p (a s) -> p a s", a=2), ys, ys, ALU.mult).then_inc(sq_ok, 1)

            def make_bias(layer, m):
                M = 16 * layer + m
                if M >= 2:
                    pool.wait_ge(logit_ok, M - 1)
                mask = dilated if layer == 0 and m >= 8 else causal
                nc.gpsimd.tensor_scalar(bias[:, M % 2, :], dist, slope(layer, m), 0.0, ALU.mult, ALU.add).then_inc(slope_ok, 1)
                pool.wait_ge(slope_ok, M + 1)
                nc.gpsimd.tensor_tensor(bias[:, M % 2, :], bias[:, M % 2, :], mask, ALU.add).then_inc(bias_ok, 1)

            pool.wait_ge(vec_c, 2)
            for layer in range(LAYERS):
                for h in range(SLOTS):
                    square(layer, h + 1)
                    for m in maps_at(layer, h + 1):
                        make_bias(layer, m)
                    if layer == 0 and h < 32:
                        i, part = h // 4, h % 4
                        w = raw[:, place["mod_g", i] % RAW, :, :]
                        if part == 0:
                            wait_raw(pool, ("mod_g", i))
                            if i:
                                pool.wait_ge(mod_T, 4 + i)
                        for k in (2 * part, 2 * part + 1):
                            done = 2 * KB * i + 2 * k
                            if k == 0:
                                nc.gpsimd.tensor_scalar(acc_g[:, :], w[:, 0, :], v[:, V_CACT:V_CACT + 1], 0.0,
                                                        ALU.mult, ALU.add).then_inc(pool_step, 2)
                                continue
                            nc.gpsimd.tensor_scalar(w[:, k, :], w[:, k, :], v[:, V_CACT + k:V_CACT + k + 1], 0.0,
                                                    ALU.mult, ALU.add).then_inc(pool_step, 1)
                            pool.wait_ge(pool_step, done + 1)
                            s = nc.gpsimd.tensor_tensor(acc_g[:, :], acc_g[:, :], w[:, k, :], ALU.add)
                            s.then_inc(pool_step, 1)

        @block.tensor
        def _(pe):
            def mm(o, a, b, start, stop):
                return nc.tensor.matmul(o, a, b, start=start, stop=stop, skip_group_check=True)

            def mm3(o, a_hi, a_lo, b_hi, b_lo, start, stop):
                mm(o, a_hi, b_hi, start, False)
                mm(o, a_hi, b_lo, False, False)
                return mm(o, a_lo, b_hi, False, stop)

            def mod_columns(acc, layer, i):
                for f in range(4):
                    o = 32 * layer + 4 * i + f
                    s = mm(small[:, o:o + 1], acc[:, f * P:(f + 1) * P], v[:, V_EPS + 1:V_EPS + 2], True, True)
                s.then_inc(mod_T, 1)

            pe.wait_ge(cst_in, 16)
            pe.wait_ge(vec_in, 16 * 16)
            nc.tensor.transpose(small[:, P:P + P], rows[:, :], ident).then_inc(cols_T, 1)
            pe.wait_ge(x_in, 16)
            for i in range(4):
                if i >= 2:
                    pe.wait_ge(xT_ok, i - 1)
                for a in range(2):
                    for t in range(2):
                        s = nc.tensor.transpose(proj[i % 2][:, a * S + t * P:a * S + (t + 1) * P],
                                                x_tok[:, t, (2 * i + a) * P:(2 * i + a + 1) * P], ident)
                s.then_inc(xT_T, 1)
            pe.wait_ge(cols_ok, 1)
            for i in range(4):
                pe.wait_ge(mod_v, i + 1)
                mod_columns(acc_v, 0, i)

            def mean_squares(j, kind):
                if j:
                    pe.wait_ge(nt_ok, j)
                pe.wait_ge(sq_ok, SQUARED[j])
                ones = head_mean if kind == "unit" else mean128
                mm(sumsq[:, :], ones, n_sq[:, :], True, True).then_inc(ssq_ok, 1)

            def turn(layer, m, t):
                M = 16 * layer + m
                pe.wait_ge(prob_ok, M + 1)
                if t:
                    pe.wait_ge(probsT_ok, t)
                for b in range(3):
                    s = nc.tensor.transpose(turned[:, b * P:(b + 1) * P], probs[:, M % 3, b * P:(b + 1) * P], ident)
                s.then_inc(turn_ok, 1)

            def mix(layer, m, t):
                grp, wide = m // 8, layer == 0 and m < 8
                hh = m % 8
                if wide:
                    o, f = mixed[:, :], slice(P * (hh // 2), P * (hh // 2) + P)
                else:
                    o, f = mixed[HD * (hh % 2):HD * (hh % 2) + HD, :], slice(HD * hh, HD * hh + HD)
                if wide or m % 2 == 0:
                    pe.wait_ge(y_raw, 8 * layer + m // 2)
                mm(o[:, 0:S], val[:, grp, 0, f], probsT[:, t % 2, 0:S], True, False)
                mm(o[:, P:S], val[:, grp, 1, f], probsT[:, t % 2, S:MAPW], False, True).then_inc(pv_ok, 1)

            def scores(layer, m):
                M = 16 * layer + m
                grp, hh = m // 8, m % 8
                if m % 8 == 0:
                    pe.wait_ge(norm_ok, max(j for j in UNIT_NORMS if NORMS[j][0] == layer and NORMS[j][3] // 6 == grp) + 1)
                if M >= 2:
                    pe.wait_ge(logit_ok, M - 1)
                q, k = qZ[:, grp, hh, :], kT[:, grp, hh // 2, :]
                mm(score[M % 2][:, 0:P], q[:, 0:P], k[:, 0:P], True, True)
                mm(score[M % 2][:, P:MAPW], q[:, P:S], k[:, 0:S], True, True).then_inc(score_ok, 1)

            def stick_logits(m):
                if m == 0:
                    pe.wait_ge(free_act, frees(UNITS + 2 * Q2 + 1, False))
                    pe.wait_ge(masks_ok, 1)
                    pe.wait_ge(logit_ok, 24)
                    pe.wait_ge(probsT_ok, 20)
                if m >= 3:
                    pe.wait_ge(d_a, m - 2)
                q, k = qZ[:, 1, m, :], kT[:, 1, m // 2, :]
                mm(score[m % 3][:, 0:S], k[:, 0:P], q[:, 0:S], True, False)
                mm(score[m % 3][:, S:MAPW], k[:, P:S], q[:, P:S], False, False)
                mm(score[m % 3][:, 0:P], mask_id[:, :], mask_tri[:, :], False, False)
                mm(score[m % 3][:, S:MAPW], mask_id[:, :], mask_tri[:, :], False, False).then_inc(score_ok, 1)

            def stick_sums(m):
                pe.wait_ge(d_sp, m + 1)
                sp = probs[:, m % 3, :]
                mm(score[m % 3][:, 0:MAPW], tri, sp[:, 0:MAPW], False, False)
                mm(score[m % 3][:, P:S], neg, sp[:, S:MAPW], False, True).then_inc(d_tri, 1)

            def project(layer, h):
                u, half = h // 2, h % 2
                n = UNITS * layer + u
                b, wh, wl = proj[n % 2], w_hi[:, n % 2, :, :], w_lo[:, n % 2, :, :]
                if half == 0:
                    pe.wait_ge(lo_done, 2 * n + 2)
                    if n == 0:
                        pe.wait_ge(xT_ok, 4)
                    elif n == 1:
                        pass
                    elif freed_by_vector(n - 2):
                        pe.wait_ge(free_dve, frees(n - 2, True))
                    else:
                        pe.wait_ge(free_act, frees(n - 2, False))
                if u >= IN_UNITS:
                    ks = range(0, 6) if half == 0 else range(6, 8)
                    pe.wait_ge(y_lo_ok, 4 * layer + (3 if half == 0 else 4))
                    for fb in range(2):
                        for k in ks:
                            f = slice(fb * P, (fb + 1) * P)
                            s = mm3(b[:, fb * S:(fb + 1) * S], wh[:, k, f], wl[:, k, f], y_hi[:, k, :], y_lo[:, k, :],
                                    fb == 0 and k == 0, k == KB - 1)
                elif u // 2 in (V1, V2):
                    t = slice(half * P, (half + 1) * P)
                    for k in range(KB):
                        s = mm3(b[:, half * UNIT:(half + 1) * UNIT], h_hi[:, k, t], h_lo[:, k, t], wh[:, k, :], wl[:, k, :],
                                k == 0, k == KB - 1)
                else:
                    f = slice(half * P, (half + 1) * P)
                    for k in range(KB):
                        if u == 0:
                            pe.wait_ge(h_ok, KB * layer + k + 1)
                        s = mm3(b[:, half * S:(half + 1) * S], wh[:, k, f], wl[:, k, f], h_hi[:, k, :], h_lo[:, k, :],
                                k == 0, k == KB - 1)
                if half:
                    s.then_inc(proj_done, 1)

            def attend(layer, h):
                for j, kind, _ in norm_at(layer, h):
                    mean_squares(j, kind)
                for m in maps_at(layer, h, 1):
                    t = head_of(layer, m)
                    if t is not None:
                        turn(layer, m, t)
                for m in maps_at(layer, h, 2):
                    t = head_of(layer, m)
                    if t is not None:
                        pe.wait_ge(probsT_ok, t + 1)
                        if m % 8 == (1 if layer == 0 and m < 8 else 0):
                            pe.wait_ge(free_act, frees(UNITS * layer + 2 * (V1 if m < 8 else V2) + 1, False))
                        mix(layer, m, t)
                for m in sticks_at(layer, h, TRI_LAG):
                    stick_sums(m)
                for m in sticks_at(layer, h, PV_LAG_D):
                    pe.wait_ge(d_a, m + 1)
                    if m == 0:
                        pe.wait_ge(free_act, frees(UNITS + 2 * V2 + 1, False))
                    mix(1, 8 + m, 20 + m)
                for m in maps_at(layer, h):
                    scores(layer, m)
                for m in sticks_at(layer, h):
                    stick_logits(m)
                if layer == 0:
                    for i in range(8):
                        if h == 4 * i + 5:
                            pe.wait_ge(pool_step, 2 * KB * (i + 1))
                            pe.wait_ge(mod_ok, 1 if i < 2 else 2)
                            if i < 2:
                                mod_columns(acc_g, 0, 4 + i)
                            else:
                                mod_columns(acc_g, 1, i - 2)

            for layer in range(LAYERS):
                j = norm_at(layer, -1)[0][0]
                if j:
                    pe.wait_ge(nt_ok, j)
                for k in range(KB):
                    if k % 2 == 0:
                        pe.wait_ge(xsq, 4 * layer + k // 2 + 1)
                    s = mm(sumsq[:, 0:S], mean, gates[:, k, :], k == 0, k == KB - 1)
                s.then_inc(ssq_ok, 1)
                for h in range(SLOTS):
                    if h < 2 * IN_UNITS:
                        project(layer, h)
                        attend(layer, h)
                    else:
                        attend(layer, h)
                        project(layer, h)
            for i in range(4):
                t, half = i % 2, i // 2
                pe.wait_ge(free_dve, frees(UNITS * LAYERS - 3 + 2 * half, True))
                for f in range(4):
                    s = nc.tensor.transpose(final[i][:, f * P:(f + 1) * P],
                                            xT[:, 4 * half + f, t * P:(t + 1) * P], ident)
                s.then_inc(out_T, 1)


_INS = ["x", "c", "norm_w", "w_mod", "b_mod", "w_in", "w_out", "a_q_norm", "a_k_norm", "a_lambda", "a_subln",
        "b_q_norm", "b_k_norm", "c_q_norm", "c_k_norm"]


def constants():
    import numpy as np
    p, col = np.arange(P)[:, None], np.arange(S)[None, :]
    d = P + p - col
    count = sum(((d % dil == 0) & (d <= window)).astype(int) for window, dil in ((128, 1), (512, 4), (2048, 16)))
    inside = (d >= 0) & (count > 0)
    f = np.arange(P)[None, :]
    parts = [d, np.where(d >= 0, 0.0, MASKED), np.where(inside, -np.log(np.maximum(count, 1)), MASKED),
             p == f, (p // HD == f // HD) / HD, np.full((P, P), 1.0 / P), np.full((P, P), 1.0 / D),
             -1.0 * (p >= f), np.full((P, P), -1.0)]
    return np.concatenate([np.asarray(a, np.float32) for a in parts], axis=1)


def kernel(**inputs):
    import numpy as np
    import concourse.bacc as bacc
    from concourse.bass_utils import run_bass_kernel_spmd

    nc = bacc.Bacc("TRN2", target_bir_lowering=False, num_devices=1)
    arrays = {f"in_{name}": np.ascontiguousarray(inputs[name]) for name in _INS}
    arrays["in_constants"] = constants()
    args = [nc.dram_tensor(name, a.shape, mybir.dt.from_np(a.dtype), kind="ExternalInput").ap()
            for name, a in arrays.items()]
    out = nc.dram_tensor("out_x", (1, S, D), F32, kind="ExternalOutput").ap()
    program(nc, *args, out)
    return run_bass_kernel_spmd(nc, [arrays], core_ids=[0]).results[0]["out_x"]
```

```python
import math
from contextlib import ExitStack

import concourse.bass as bass
from concourse import mybir

F32 = mybir.dt.float32
F32R = mybir.dt.float32r
BF16 = mybir.dt.bfloat16
ALU = mybir.AluOpType
ACT = mybir.ActivationFunctionType
AX = mybir.AxisListType

P = 128
D = 1024
S = 256
LAYERS = 2
KB = D // P
HD = 64
EPS = 1e-6
SCALE = HD ** -0.5
MASKED = 1e30
LAMBDA_INIT = 0.8 - 0.6 * math.exp(-0.3 * 0)
CHUNK = 512
UNIT = 256
RAW = 3
PIECES = 4
AHEAD = 2
MAPW = 384

IN_UNITS = 16
UNITS = 20
SLOTS = 2 * UNITS
ORDER = (1, 0, 2, 5, 4, 6, 3, 7)
K1, Q1, V1, K2, Q2, V2, G1, G2 = range(8)
FIRST_MAP = (11, 23)
FIRST_D = 21
TRI_LAG, PV_LAG_D = 2, 3
GATE_AT = (28, 30, 31, 32)
SUBLN_AT = (24, 26)

MOD_CHUNKS = 8
MOD_LAG = 7
MOD_GROUPS = ((1, MOD_LAG + 4), (2, MOD_LAG + 28))

R_C, R_NORM, R_BMOD = 0, KB, KB + LAYERS * KB
R_QK = R_BMOD + LAYERS * 3 * KB
R_SUBLN = R_QK + 6
ROWS = R_SUBLN + 1

C_ID, C_MEAN, C_HEAD, C_MEAN128, C_TRI, C_NEG = (P * i for i in range(6))
C_DIST, C_CAUSAL, C_DIL = (P * 6 + S * i for i in range(3))
C_LATE = 2 * P
CONSTS = P * 6 + S * 3

V_A, V_B, V_GATE = 0, 2 * KB, 4 * KB
V_QK = 6 * KB
V_SUBLN = V_QK + 6
V_CACT = V_SUBLN + 1
V_TMP = V_CACT + KB
V_LAM = V_TMP + 8
V_EPS = V_LAM + 8
V_N = V_EPS + 2


def maps_at(layer, h, lag=0):
    h -= lag
    out = [h - FIRST_MAP[0]] if 0 <= h - FIRST_MAP[0] < 8 else []
    if layer == 0 and 0 <= h - FIRST_MAP[1] < 8:
        out.append(8 + h - FIRST_MAP[1])
    return out


def sticks_at(layer, h, lag=0):
    h -= lag
    return [h - FIRST_D] if layer == 1 and 0 <= h - FIRST_D < 8 else []


def head_of(layer, m):
    if layer == 0 and m < 8:
        return m // 2 if m % 2 else None
    return m - 4 if layer == 0 else 12 + m


def normed(layer, u):
    return u < IN_UNITS and u // 2 in ((K1, Q1, K2, Q2) if layer == 0 else (K1, Q1))


def norms():
    out = []
    for layer in range(LAYERS):
        out.append((layer, -1, "rms", 0))
        for h in range(SLOTS):
            if h % 2 and h >= 3 and normed(layer, (h - 3) // 2):
                out.append((layer, h, "unit", (h - 3) // 2))
            if layer == 0 and h in SUBLN_AT:
                out.append((layer, h, "subln", SUBLN_AT.index(h)))
    return out


NORMS = norms()


def norm_at(layer, h):
    return [(j, kind, i) for j, (la, hh, kind, i) in enumerate(NORMS) if (la, hh) == (layer, h)]


def freed_by_vector(n):
    u = n % UNITS
    return u // 2 in (G1, G2) or u >= IN_UNITS


def frees(n, vector):
    return sum(freed_by_vector(i) == vector for i in range(n + 1))


SQUARED = [sum(kind != "rms" for _, _, kind, _ in NORMS[:j + 1]) for j in range(len(NORMS))]
UNIT_NORMS = [j for j, (_, _, kind, _) in enumerate(NORMS) if kind == "unit"]


def turned_by(layer, m):
    return m // 2 + 1 if layer == 0 and m < 8 else (m - 3 if layer == 0 else 13 + m)


def slope(layer, m):
    if layer == 0 and m < 8:
        return 2.0 ** (-8.0 * (m // 2 + 1) / 4)
    return 2.0 ** (-(m % 8 + 1))


def program(nc, x, w_mod, w_in, w_out, a_lambda, vectors, consts, out):
    with ExitStack() as ctx:
        def sb(name, shape, dt=F32):
            return ctx.enter_context(nc.sbuf_tensor(name, shape, dt))

        def bank(name):
            return ctx.enter_context(nc.psum_tensor(name, [P, 512], F32))

        def sem(name):
            return ctx.enter_context(nc.semaphore(name))

        raw = sb("raw", [P, RAW, KB, CHUNK])
        w_hi = sb("w_hi", [P, PIECES, KB // 2, UNIT], F32R)
        w_lo = sb("w_lo", [P, PIECES, KB // 2, UNIT], F32R)
        h_hi = sb("h_hi", [P, KB, S], F32R)
        h_lo = sb("h_lo", [P, KB, S], F32R)
        y_hi = sb("y_hi", [P, KB, S], F32R)
        y_lo = sb("y_lo", [P, KB, S], F32R)
        xT = sb("xT", [P, KB, S])
        y = sb("y", [P, KB, S])
        gates = sb("gates", [P, KB, S])
        kT = sb("kT", [P, 2, 4, S])
        qZ = sb("qZ", [P, 2, 8, S])
        val = sb("val", [P, 2, 2, CHUNK])
        n_raw = sb("n_raw", [P, 2, 512])
        n_sq = sb("n_sq", [P, 512])
        n_y0 = sb("n_y0", [P, 512])
        n_t = sb("n_t", [P, 512])
        logits = sb("logits", [P, 2, 512])
        probs = sb("probs", [P, 3, 512])
        probsT = sb("probsT", [P, 2, 512])
        bias = sb("bias", [P, 2, S])
        lam = logits[:, 0, 0:4 * HD].rearrange("p (i d) -> p i d", i=4)
        acc_v = sb("acc_v", [P, CHUNK])
        acc_g = sb("acc_g", [P, 2, CHUNK])
        rows = sb("rows", [P, P])
        cols = sb("cols", [P, ROWS])
        v = sb("v", [P, V_N])
        cst = sb("cst", [P, CONSTS])
        mask_id = sb("mask_id", [P, P], BF16)
        mask_tri = sb("mask_tri", [P, P], BF16)
        stat = sb("stat", [P, 2, 8])

        dist, causal, dilated = (cst[:, o:o + S] for o in (C_DIST, C_CAUSAL, C_DIL))
        ident, head_mean, mean128, mean, tri, neg = (
            cst[:, o:o + P] for o in (C_ID, C_HEAD, C_MEAN128, C_MEAN, C_TRI, C_NEG))
        x_tok = y[:, :, :].rearrange("p a b -> p (a b)").rearrange("p (t f) -> p t f", t=2)
        out_tok = x_tok

        proj = [bank("proj0"), bank("proj1")]
        sumsq = bank("sumsq")
        score = [bank("score0"), bank("score1"), bank("turned")]
        turned = score[2]
        mixed = bank("mixed")
        final = score + [mixed]
        small = bank("small")

        raw_full = [sem(f"raw_full{i}") for i in range(RAW)]
        x_in, vec_in, lam_in = sem("x_in"), sem("vec_in"), sem("lam_in")
        cst_in, late_in = sem("cst_in"), sem("late_in")
        masks_ok = sem("masks_ok")
        zeroed = sem("zeroed")
        cols_T, cols_ok = sem("cols_T"), sem("cols_ok")
        act_c = sem("act_c")
        vec_c = sem("vec_c")
        xT_T, xT_ok = sem("xT_T"), sem("xT_ok")
        mod_v = sem("mod_v")
        mod_part = sem("mod_part")
        mod_T, mod_ok = sem("mod_T"), sem("mod_ok")
        hi_done, lo_done = sem("hi_done"), sem("lo_done")
        xsq = sem("xsq")
        h_pre, h_hi_ok, h_ok = sem("h_pre"), sem("h_hi_ok"), sem("h_ok")
        half_done = sem("half_done")
        free_act, free_dve = sem("free_act"), sem("free_dve")
        sq_ok, ssq_ok = sem("sq_ok"), sem("ssq_ok")
        ln_ok, y0_ok = sem("ln_ok"), sem("y0_ok")
        nt_ok, norm_ok = sem("nt_ok"), sem("norm_ok")
        g_step, ln_sigmoid = sem("g_step"), sem("ln_sigmoid")
        slope_ok, bias_ok = sem("slope_ok"), sem("bias_ok")
        score_ok, logit_ok, exp_ok, prob_ok = (sem(n) for n in ("score_ok", "logit_ok", "exp_ok", "prob_ok"))
        turn_ok, probsT_ok, pv_ok, y_raw = (sem(n) for n in ("turn_ok", "probsT_ok", "pv_ok", "y_raw"))
        d_abs, d_exp, d_ln, d_sp = (sem(n) for n in ("d_abs", "d_exp", "d_ln", "d_sp"))
        d_tri, d_a = sem("d_tri"), sem("d_a")
        y_ok, y_hi_ok, y_lo_ok = sem("y_ok"), sem("y_hi_ok"), sem("y_lo_ok")
        out_T, out_ok, stored = sem("out_T"), sem("out_ok"), sem("stored")
        pool_step = sem("pool_step")
        dve_step = sem("dve_step")

        chunks = [("mod_v", i) for i in range(4)]
        for i in range(8):
            chunks += [("w", i), ("mod_g", i)]
        chunks += [("w", i) for i in range(8, UNITS)]
        place = {key: n for n, key in enumerate(chunks)}

        def source(kind, i):
            if kind == "mod_v":
                w, col = w_mod[0], CHUNK * i
            elif kind == "mod_g":
                w, col = (w_mod[0], CHUNK * (4 + i)) if i < 2 else (w_mod[1], CHUNK * (i - 2))
            elif i % 10 < 8:
                w, col = w_in[i // 10], CHUNK * ORDER[i % 10]
            else:
                w, col = w_out[i // 10], CHUNK * (i % 10 - 8)
            return w[:, col:col + CHUNK].rearrange("(k p) n -> p k n", p=P)

        def wait_raw(eng, key):
            n = place[key]
            eng.wait_ge(raw_full[n % RAW], 16 * (n // RAW + 1))

        block = ctx.enter_context(nc.Block())

        @block.sync
        def _(sp):
            def load(n):
                kind, i = chunks[n]
                if n >= RAW:
                    was, j = chunks[n - RAW]
                    if was == "mod_v":
                        sp.wait_ge(mod_v, j + 1)
                    elif was == "mod_g":
                        sp.wait_ge(pool_step, 9 * (j + 1))
                    else:
                        sp.wait_ge(lo_done, 4 * (j + 1))
                sp.dma_start(raw[:, n % RAW, :, :], source(kind, i)).then_inc(raw_full[n % RAW], 16)

            sp.dma_start(rows[:, :], vectors).then_inc(vec_in, 16)
            sp.dma_start(lam, a_lambda.rearrange("a i d -> a (i d)").broadcast_to([P, 4 * HD])
                         .rearrange("p (i d) -> p i d", i=4)).then_inc(lam_in, 16)
            sp.dma_start(cst[:, 0:C_LATE], consts[:, 0:C_LATE]).then_inc(cst_in, 16)
            load(0)
            sp.dma_start(x_tok, x[0].rearrange("(t p) f -> p t f", p=P)).then_inc(x_in, 16)
            for n in range(1, len(chunks)):
                load(n)
                if chunks[n] == ("w", 0):
                    sp.dma_start(cst[:, C_LATE:], consts[:, C_LATE:]).then_inc(late_in, 16)
            for i in range(4):
                t, half = i % 2, i // 2
                sp.wait_ge(out_ok, i + 1)
                sp.dma_start(out[0, t * P:(t + 1) * P, half * 512:(half + 1) * 512],
                             out_tok[:, t, half * 512:(half + 1) * 512]).then_inc(stored, 16)
            sp.wait_ge(stored, 64)

        @block.scalar
        def _(act):
            act.preload_act_table_set("natural_log_exp_and_others")
            act.wait_ge(cols_ok, 1)
            nc.scalar.activation(v[:, V_CACT:V_CACT + KB], cols[:, R_C:R_C + KB], ACT.Exp, scale=-1.0).then_inc(act_c, 1)
            act.wait_ge(vec_c, 1)
            nc.scalar.activation(v[:, V_LAM + 2:V_LAM + 4], v[:, V_LAM:V_LAM + 2], ACT.Exp).then_inc(act_c, 1)

            for i in range(4):
                act.wait_ge(xT_T, i + 1)
                nc.scalar.activation(xT[:, 2 * i:2 * i + 2, :], proj[i % 2][:, :], ACT.Copy).then_inc(xT_ok, 1)

            def split_hi(piece):
                n, half = piece // 2, piece % 2
                wait_raw(act, ("w", n // 2))
                if piece >= PIECES:
                    act.wait_ge(half_done, piece - PIECES + 1)
                nc.scalar.activation(w_hi[:, piece % PIECES, :, :],
                                     raw[:, place["w", n // 2] % RAW, 4 * half:4 * half + 4,
                                         (n % 2) * UNIT:(n % 2 + 1) * UNIT],
                                     ACT.Copy).then_inc(hi_done, 1)

            def norm_seed(j, width):
                act.wait_ge(ssq_ok, j + 1)
                if j:
                    act.wait_ge(norm_ok, j)
                nc.scalar.activation(n_y0[:, 0:width], sumsq[:, 0:width], ACT.Ln,
                                     bias=v[:, V_EPS:V_EPS + 1]).then_inc(ln_ok, 1)
                act.wait_ge(ln_ok, j + 1)
                nc.scalar.activation(n_y0[:, 0:width], n_y0[:, 0:width], ACT.Exp, scale=-0.5).then_inc(y0_ok, 1)

            def take_unit(layer, u):
                n = UNITS * layer + u
                group, part = u // 2, u % 2
                b = proj[n % 2]
                act.wait_ge(half_done, 2 * n + 2)
                if normed(layer, u):
                    r = UNIT_NORMS.index(norm_of[layer, u])
                    if r >= 2:
                        act.wait_ge(norm_ok, UNIT_NORMS[r - 2] + 1)
                    nc.scalar.activation(n_raw[:, r % 2, :], b[:, :], ACT.Copy).then_inc(free_act, 1)
                elif group in (V1, V2):
                    nc.scalar.activation(val[:, int(group == V2), :, part * UNIT:(part + 1) * UNIT],
                                         b[:, :].rearrange("p (t n) -> p t n", t=2), ACT.Copy).then_inc(free_act, 1)
                elif group == K2:
                    nc.scalar.activation(kT[:, 1, 2 * part:2 * part + 2, :],
                                         b[:, :].rearrange("p (a s) -> p a s", a=2), ACT.Copy).then_inc(free_act, 1)
                elif group == Q2:
                    act.wait_ge(zeroed, 4)
                    for odd in range(2):
                        half = slice(HD * odd, HD * odd + HD)
                        i = nc.scalar.activation(qZ[half, 1, 4 * part + odd:4 * part + 4:2, :],
                                                 b[half, :].rearrange("p (a s) -> p a s", a=2), ACT.Copy, scale=SCALE)
                    i.then_inc(free_act, 1)
                else:
                    i = 2 * (group - G1) + part
                    act.wait_ge(h_ok, KB * (layer + 1))
                    nc.scalar.activation(gates[:, 2 * i:2 * i + 2, :],
                                         b[:, :].rearrange("p (a s) -> p a s", a=2), ACT.Abs).then_inc(g_step, 1)
                    g, steps = gates[:, 2 * i:2 * i + 2, :], 4 * (4 * layer + i)
                    act.wait_ge(g_step, steps + 1)
                    nc.scalar.activation(g, g, ACT.Exp, scale=-1.0).then_inc(g_step, 1)
                    act.wait_ge(g_step, steps + 2)
                    nc.scalar.activation(g, g, ACT.Ln, bias=1.0).then_inc(g_step, 1)

            def take_gates(layer, i):
                g = gates[:, 2 * i:2 * i + 2, :]
                act.wait_ge(ln_sigmoid, 4 * layer + i + 1)
                nc.scalar.activation(g, g, ACT.Exp).then_inc(g_step, 1)

            norm_of = {(la, i): j for j, (la, _, kind, i) in enumerate(NORMS) if kind == "unit"}

            for piece in range(AHEAD):
                split_hi(piece)
            for layer in range(LAYERS):
                for i in range(4):
                    if layer:
                        act.wait_ge(free_dve, frees(UNITS * layer - 4 + i, True))
                        act.wait_ge(y_ok, 4 * layer)
                    else:
                        act.wait_ge(xT_ok, i + 1)
                    nc.scalar.activation(gates[:, 2 * i:2 * i + 2, :], xT[:, 2 * i:2 * i + 2, :], ACT.Square).then_inc(xsq, 1)
                norm_seed(norm_at(layer, -1)[0][0], S)
                for k in range(KB):
                    act.wait_ge(h_pre, KB * layer + k + 1)
                    nc.scalar.activation(h_hi[:, k, :], gates[:, k, :], ACT.Identity,
                                         bias=v[:, V_B + KB * layer + k:V_B + KB * layer + k + 1]).then_inc(h_hi_ok, 1)
                for h in range(SLOTS):
                    n = UNITS * layer + h // 2
                    if h % 2 and h < 2 * IN_UNITS:
                        take_unit(layer, h // 2)
                    if h % 2 == 0 and 2 * G1 < h // 2 <= IN_UNITS:
                        take_gates(layer, h // 2 - 1 - 2 * G1)
                    for j, _, _ in norm_at(layer, h):
                        norm_seed(j, 512)
                    for m in maps_at(layer, h, 1):
                        t = head_of(layer, m)
                        if t is not None:
                            act.wait_ge(turn_ok, t + 1)
                            if t >= 2:
                                act.wait_ge(pv_ok, t - 1)
                            nc.scalar.activation(probsT[:, t % 2, 0:MAPW], turned[:, 0:MAPW], ACT.Copy).then_inc(probsT_ok, 1)
                    if SLOTS * layer + h + AHEAD < SLOTS * LAYERS:
                        split_hi(SLOTS * layer + h + AHEAD)
                    for m in maps_at(layer, h, 2):
                        t = head_of(layer, m)
                        if t is not None and (layer == 0 and m < 8 or m % 2):
                            blk = m // 2
                            act.wait_ge(pv_ok, t + 1)
                            nc.scalar.activation(y[:, blk, :], mixed[:, 0:S], ACT.Copy).then_inc(y_raw, 1)
                    for m in sticks_at(layer, h, TRI_LAG):
                        act.wait_ge(d_tri, m + 1)
                        act.wait_ge(pv_ok, 20 + m - 1)
                        nc.scalar.activation(probsT[:, m % 2, 0:MAPW], score[m % 3][:, 0:MAPW], ACT.Exp).then_inc(d_a, 1)
                    for m in sticks_at(layer, h, PV_LAG_D):
                        if m % 2:
                            act.wait_ge(pv_ok, 20 + m + 1)
                            nc.scalar.activation(y[:, 4 + m // 2, :], mixed[:, 0:S], ACT.Copy).then_inc(y_raw, 1)
                    for m in maps_at(layer, h):
                        M = 16 * layer + m
                        act.wait_ge(logit_ok, M + 1)
                        if M >= 2:
                            act.wait_ge(prob_ok, M - 1)
                        if M >= 3:
                            act.wait_ge(turn_ok, turned_by((M - 3) // 16, (M - 3) % 16))
                        for tile, cs in enumerate((slice(0, P), slice(P, MAPW))):
                            i = nc.scalar.activation(probs[:, M % 3, cs], logits[:, M % 2, cs], ACT.Exp, scale=-1.0,
                                                     bias=stat[:, M % 2, tile:tile + 1],
                                                     accum_out=stat[:, M % 2, 2 + tile:3 + tile])
                        i.then_inc(exp_ok, 1)
                    for m in sticks_at(layer, h):
                        act.wait_ge(score_ok, 24 + m + 1)
                        act.wait_ge(d_sp, m - 1) if m >= 2 else act.wait_ge(prob_ok, 24)
                        nc.scalar.activation(logits[:, m % 2, 0:MAPW], score[m % 3][:, 0:MAPW], ACT.Abs).then_inc(d_abs, 1)
                        act.wait_ge(d_abs, m + 1)
                        nc.scalar.activation(logits[:, m % 2, 0:MAPW], logits[:, m % 2, 0:MAPW], ACT.Exp, scale=-1.0).then_inc(d_exp, 1)
                        act.wait_ge(d_exp, m + 1)
                        nc.scalar.activation(logits[:, m % 2, 0:MAPW], logits[:, m % 2, 0:MAPW], ACT.Ln, bias=1.0).then_inc(d_ln, 1)
                    if h in GATE_AT:
                        i = GATE_AT.index(h)
                        act.wait_ge(y_ok, 4 * layer + i + 1)
                        nc.scalar.activation(y_hi[:, 2 * i:2 * i + 2, :], y[:, 2 * i:2 * i + 2, :], ACT.Copy).then_inc(y_hi_ok, 1)
            for i in range(4):
                act.wait_ge(out_T, i + 1)
                nc.scalar.activation(out_tok[:, i % 2, (i // 2) * 512:(i // 2 + 1) * 512],
                                     final[i][:, :], ACT.Copy).then_inc(out_ok, 1)

        @block.vector
        def _(dve):
            steps = [0]

            def link(ins):
                steps[0] += 1
                ins.then_inc(dve_step, 1)
                dve.wait_ge(dve_step, steps[0])

            def col(i, n=1):
                return v[:, i:i + n]

            nc.vector.memset(col(V_EPS), EPS)
            nc.vector.memset(col(V_EPS + 1), 1.0)

            dve.wait_ge(cols_T, 1)
            nc.vector.tensor_copy(cols[:, :], small[:, P:P + ROWS]).then_inc(cols_ok, 1)
            dve.wait_ge(lam_in, 16)
            for i in range(2):
                j = nc.vector.tensor_tensor_reduce(out=n_t[:, 0:HD], in0=lam[:, 2 * i, :], in1=lam[:, 2 * i + 1, :],
                                                   scale=1.0, scalar=0.0, op0=ALU.mult, op1=ALU.add,
                                                   accum_out=col(V_LAM + i))
                if i == 0:
                    link(j)
            j.then_inc(vec_c, 1)
            dve.wait_ge(act_c, 1)
            dve.wait_ge(cols_ok, 1)
            link(nc.vector.tensor_scalar_add(col(V_CACT, KB), col(V_CACT, KB), 1.0))
            link(nc.vector.reciprocal(col(V_CACT, KB), col(V_CACT, KB)))
            nc.vector.tensor_tensor(col(V_CACT, KB), col(V_CACT, KB), cols[:, R_C:R_C + KB], ALU.mult).then_inc(vec_c, 1)
            dve.wait_ge(act_c, 2)
            nc.vector.scalar_tensor_tensor(out=col(V_LAM + 4), in0=col(V_LAM + 3), scalar=-LAMBDA_INIT,
                                           in1=col(V_LAM + 2), op0=ALU.add, op1=ALU.subtract)
            for i in range(6):
                f = 0.5 * SCALE if i % 2 == 0 else -0.5
                nc.vector.tensor_scalar_mul(col(V_QK + i), cols[:, R_QK + i:R_QK + i + 1], f)
            link(nc.vector.tensor_scalar_mul(col(V_SUBLN), cols[:, R_SUBLN:R_SUBLN + 1], -0.5 * (1.0 - LAMBDA_INIT)))

            dve.wait_ge(vec_c, 2)
            for i in range(4):
                wait_raw(dve, ("mod_v", i))
                if i:
                    dve.wait_ge(mod_T, i)
                w = raw[:, place["mod_v", i] % RAW, :, :]
                link(nc.vector.tensor_scalar_mul(acc_v[:, :], w[:, 0, :], col(V_CACT)))
                for k in range(1, KB):
                    j = nc.vector.scalar_tensor_tensor(out=acc_v[:, :], in0=w[:, k, :], scalar=col(V_CACT + k),
                                                       in1=acc_v[:, :], op0=ALU.mult, op1=ALU.add)
                    if k < KB - 1:
                        link(j)
                j.then_inc(mod_v, 1)

            def take_shift_scale(layer):
                o = 32 * layer
                b = R_BMOD + 3 * KB * layer
                nw = R_NORM + KB * layer
                nc.vector.tensor_tensor(col(V_B + KB * layer, KB), small[:, o:o + KB], cols[:, b:b + KB], ALU.add)
                link(nc.vector.tensor_tensor(col(V_TMP, KB), small[:, o + KB:o + 2 * KB],
                                             cols[:, b + KB:b + 2 * KB], ALU.add))
                link(nc.vector.scalar_tensor_tensor(out=col(V_TMP, KB), in0=col(V_TMP, KB), scalar=1.0,
                                                    in1=cols[:, nw:nw + KB], op0=ALU.add, op1=ALU.mult))
                return nc.vector.tensor_scalar_mul(col(V_A + KB * layer, KB), col(V_TMP, KB), -0.5)

            def take_gate(layer):
                o = 32 * layer + 2 * KB
                b = R_BMOD + 3 * KB * layer + 2 * KB
                return nc.vector.tensor_tensor(col(V_GATE + KB * layer, KB), small[:, o:o + KB],
                                               cols[:, b:b + KB], ALU.add)

            dve.wait_ge(mod_T, 4)
            take_shift_scale(0).then_inc(mod_ok, 1)
            dve.wait_ge(mod_ok, 1)

            def split_lo(piece):
                n, half = piece // 2, piece % 2
                dve.wait_ge(hi_done, piece + 1)
                nc.vector.tensor_tensor(w_lo[:, piece % PIECES, :, :],
                                        raw[:, place["w", n // 2] % RAW, 4 * half:4 * half + 4,
                                            (n % 2) * UNIT:(n % 2 + 1) * UNIT],
                                        w_hi[:, piece % PIECES, :, :], ALU.subtract).then_inc(lo_done, 1)

            def refine(j, width):
                dve.wait_ge(y0_ok, j + 1)
                nc.vector.scalar_tensor_tensor(out=n_t[:, 0:width], in0=sumsq[:, 0:width], scalar=EPS,
                                               in1=n_y0[:, 0:width], op0=ALU.add, op1=ALU.mult).then_inc(nt_ok, 1)
                dve.wait_ge(nt_ok, j + 1)
                link(nc.vector.tensor_tensor(n_t[:, 0:width], n_t[:, 0:width], n_y0[:, 0:width], ALU.mult))
                link(nc.vector.scalar_tensor_tensor(out=n_t[:, 0:width], in0=n_t[:, 0:width], scalar=-3.0,
                                                    in1=n_y0[:, 0:width], op0=ALU.add, op1=ALU.mult))

            def norm_unit(j, layer, u):
                refine(j, 512)
                r = UNIT_NORMS.index(j)
                grp, part = u // 6, u % 2
                is_k = u // 2 in (K1, K2)
                w = V_QK + 4 * layer + 2 * grp + is_k
                if is_k:
                    i = nc.vector.scalar_tensor_tensor(
                        out=kT[:, grp, 2 * part:2 * part + 2, :],
                        in0=n_raw[:, r % 2, :].rearrange("p (a s) -> p a s", a=2), scalar=col(w),
                        in1=n_t[:, :].rearrange("p (a s) -> p a s", a=2), op0=ALU.mult, op1=ALU.mult)
                else:
                    dve.wait_ge(zeroed, 4)
                    for odd in range(2):
                        half = slice(HD * odd, HD * odd + HD)
                        i = nc.vector.scalar_tensor_tensor(
                            out=qZ[half, grp, 4 * part + odd:4 * part + 4:2, :],
                            in0=n_raw[half, r % 2, :].rearrange("p (a s) -> p a s", a=2), scalar=v[half, w:w + 1],
                            in1=n_t[half, :].rearrange("p (a s) -> p a s", a=2), op0=ALU.mult, op1=ALU.mult)
                i.then_inc(norm_ok, 1)

            def norm_subln(j, i):
                refine(j, 512)
                nc.vector.scalar_tensor_tensor(
                    out=y[:, 2 * i:2 * i + 2, :], in0=y[:, 2 * i:2 * i + 2, :], scalar=col(V_SUBLN),
                    in1=n_t[:, :].rearrange("p (a s) -> p a s", a=2), op0=ALU.mult, op1=ALU.mult).then_inc(norm_ok, 1)

            for piece in range(AHEAD):
                split_lo(piece)
            for layer in range(LAYERS):
                j = norm_at(layer, -1)[0][0]
                refine(j, S)
                for k in range(KB + 1):
                    if k < KB:
                        nc.vector.scalar_tensor_tensor(
                            out=gates[:, k, :], in0=xT[:, k, :], scalar=col(V_A + KB * layer + k),
                            in1=n_t[:, 0:S], op0=ALU.mult, op1=ALU.mult).then_inc(h_pre, 1)
                    if k:
                        dve.wait_ge(h_hi_ok, KB * layer + k)
                        nc.vector.scalar_tensor_tensor(
                            out=h_lo[:, k - 1, :], in0=gates[:, k - 1, :], scalar=col(V_B + KB * layer + k - 1),
                            in1=h_hi[:, k - 1, :], op0=ALU.add, op1=ALU.subtract).then_inc(h_ok, 1)
                dve.wait_ge(h_ok, KB * (layer + 1))
                nc.vector.tensor_copy(col(V_TMP), col(V_EPS)).then_inc(norm_ok, 1)
                if layer:
                    nc.vector.tensor_scalar_mul(mask_id[:, :], ident, MASKED)
                    nc.vector.tensor_copy(mask_tri[:, :], tri).then_inc(masks_ok, 1)
                for h in range(SLOTS):
                    u = h // 2
                    n = UNITS * layer + u
                    for j, kind, i in norm_at(layer, h - 1) if h else []:
                        if kind == "unit":
                            norm_unit(j, layer, i)
                        else:
                            norm_subln(j, i)
                    if h % 2 and u < IN_UNITS and u // 2 in (G1, G2):
                        i = u - 2 * G1
                        g = gates[:, 2 * i:2 * i + 2, :]
                        dve.wait_ge(g_step, 4 * (4 * layer + i) + 3)
                        nc.vector.scalar_tensor_tensor(
                            out=g, in0=proj[n % 2][:, :].rearrange("p (a s) -> p a s", a=2), scalar=0.0, in1=g,
                            op0=ALU.min, op1=ALU.subtract).then_inc(ln_sigmoid, 1)
                    if h % 2 == 0 and 2 * G1 < u <= IN_UNITS:
                        i = u - 1 - 2 * G1
                        g = gates[:, 2 * i:2 * i + 2, :]
                        dve.wait_ge(g_step, 4 * (4 * layer + i) + 4)
                        nc.vector.tensor_tensor(g, proj[(n - 1) % 2][:, :].rearrange("p (a s) -> p a s", a=2), g,
                                                ALU.mult).then_inc(free_dve, 1)
                        dve.wait_ge(free_dve, frees(n - 1, True))
                    if h % 2 and u >= IN_UNITS:
                        i = u - IN_UNITS
                        dve.wait_ge(half_done, 2 * n + 2)
                        for fb in range(2):
                            k = 2 * i + fb
                            s = nc.vector.scalar_tensor_tensor(
                                out=xT[:, k, :], in0=proj[n % 2][:, fb * S:(fb + 1) * S],
                                scalar=col(V_GATE + KB * layer + k), in1=xT[:, k, :], op0=ALU.mult, op1=ALU.add)
                        s.then_inc(free_dve, 1)
                    for m in maps_at(layer, h):
                        M = 16 * layer + m
                        dve.wait_ge(score_ok, M + 1)
                        dve.wait_ge(bias_ok, M + 1)
                        if M >= 2:
                            dve.wait_ge(exp_ok, M - 1)
                        for tile, (cs, bs) in enumerate(((slice(0, P), slice(P, S)), (slice(P, MAPW), slice(0, S)))):
                            i = nc.vector.tensor_tensor_reduce(
                                out=logits[:, M % 2, cs], in0=score[M % 2][:, cs], in1=bias[:, M % 2, bs],
                                scale=1.0, scalar=3e38, op0=ALU.add, op1=ALU.min,
                                accum_out=stat[:, M % 2, tile:tile + 1])
                        i.then_inc(logit_ok, 1)
                    if h in GATE_AT:
                        i = GATE_AT.index(h)
                        ys = y[:, 2 * i:2 * i + 2, :]
                        dve.wait_ge(y_raw, 8 * layer + 2 * i + 2)
                        nc.vector.tensor_tensor(ys, ys, gates[:, 2 * i:2 * i + 2, :], ALU.mult).then_inc(y_ok, 1)
                    if SLOTS * layer + h + AHEAD < SLOTS * LAYERS:
                        split_lo(SLOTS * layer + h + AHEAD)
                    if layer == 0 and h < 4 * MOD_CHUNKS:
                        i, k = h // 4, 4 + h % 4
                        w = raw[:, place["mod_g", i] % RAW, k, :]
                        if k == 4:
                            wait_raw(dve, ("mod_g", i))
                            if i:
                                dve.wait_ge(pool_step, 9 * i)
                            link(nc.vector.tensor_scalar_mul(acc_v[:, :], w, col(V_CACT + k)))
                        else:
                            j = nc.vector.scalar_tensor_tensor(out=acc_v[:, :], in0=w, scalar=col(V_CACT + k),
                                                               in1=acc_v[:, :], op0=ALU.mult, op1=ALU.add)
                            if k < KB - 1:
                                link(j)
                            else:
                                j.then_inc(mod_part, 1)
                    for m in maps_at(layer, h):
                        M = 16 * layer + m
                        dve.wait_ge(exp_ok, M + 1)
                        st = stat[:, M % 2, :]
                        link(nc.vector.reciprocal(st[:, 4:6], st[:, 2:4]))
                        for tile, cs in enumerate((slice(0, P), slice(P, MAPW))):
                            if layer == 0 and m < 8 and m % 2:
                                if tile == 0:
                                    link(nc.vector.tensor_scalar_mul(st[:, 6:8], st[:, 4:6], col(V_LAM + 4)))
                                i = nc.vector.scalar_tensor_tensor(
                                    out=probs[:, M % 3, cs], in0=probs[:, M % 3, cs], scalar=st[:, 6 + tile:7 + tile],
                                    in1=probs[:, (M - 1) % 3, cs], op0=ALU.mult, op1=ALU.add)
                            else:
                                i = nc.vector.tensor_scalar_mul(probs[:, M % 3, cs], probs[:, M % 3, cs],
                                                                st[:, 4 + tile:5 + tile])
                        i.then_inc(prob_ok, 1)
                        dve.wait_ge(prob_ok, M + 1)
                    for m in sticks_at(layer, h):
                        dve.wait_ge(d_ln, m + 1)
                        if m >= 3:
                            dve.wait_ge(d_tri, m - 2)
                        else:
                            dve.wait_ge(turn_ok, 20)
                        nc.vector.scalar_tensor_tensor(
                            out=probs[:, m % 3, 0:MAPW], in0=score[m % 3][:, 0:MAPW], scalar=0.0,
                            in1=logits[:, m % 2, 0:MAPW], op0=ALU.max, op1=ALU.add).then_inc(d_sp, 1)
                    if h in GATE_AT:
                        i = GATE_AT.index(h)
                        dve.wait_ge(y_hi_ok, 4 * layer + i + 1)
                        nc.vector.tensor_tensor(y_lo[:, 2 * i:2 * i + 2, :], y[:, 2 * i:2 * i + 2, :],
                                                y_hi[:, 2 * i:2 * i + 2, :], ALU.subtract).then_inc(y_lo_ok, 1)
                    if layer == 0 and h == MOD_GROUPS[0][1]:
                        dve.wait_ge(mod_T, 6)
                        take_gate(0).then_inc(mod_ok, 1)
                    if layer == 0 and h == MOD_GROUPS[1][1]:
                        dve.wait_ge(mod_T, 12)
                        take_shift_scale(1)
                        take_gate(1).then_inc(mod_ok, 1)
                        dve.wait_ge(mod_ok, 3)

        @block.gpsimd
        def _(pool):
            for grp in range(2):
                for odd in range(2):
                    nc.gpsimd.memset(qZ[HD * (1 - odd):HD * (2 - odd), grp, odd::2, :], 0.0).then_inc(zeroed, 1)
                    pool.wait_ge(zeroed, 2 * grp + odd + 1)
            pool.wait_ge(late_in, 16)

            def square(layer, h):
                for j, kind, i in norm_at(layer, h):
                    pool.wait_ge(ssq_ok, j)
                    if kind == "unit":
                        r = UNIT_NORMS.index(j)
                        n = UNITS * layer + i
                        pool.wait_ge(free_act, frees(n, False))
                        nc.gpsimd.tensor_tensor(n_sq[:, :], n_raw[:, r % 2, :], n_raw[:, r % 2, :], ALU.mult).then_inc(sq_ok, 1)
                    else:
                        ys = y[:, 2 * i:2 * i + 2, :]
                        pool.wait_ge(y_raw, 2 * i + 2)
                        nc.gpsimd.tensor_tensor(n_sq[:, :].rearrange("p (a s) -> p a s", a=2), ys, ys, ALU.mult).then_inc(sq_ok, 1)

            def make_bias(layer, m):
                M = 16 * layer + m
                if M >= 2:
                    pool.wait_ge(logit_ok, M - 1)
                mask = dilated if layer == 0 and m >= 8 else causal
                nc.gpsimd.tensor_scalar(bias[:, M % 2, :], dist, slope(layer, m), 0.0, ALU.mult, ALU.add).then_inc(slope_ok, 1)
                pool.wait_ge(slope_ok, M + 1)
                nc.gpsimd.tensor_tensor(bias[:, M % 2, :], bias[:, M % 2, :], mask, ALU.add).then_inc(bias_ok, 1)

            pool.wait_ge(vec_c, 2)
            for layer in range(LAYERS):
                for h in range(SLOTS):
                    square(layer, h + 1)
                    for m in maps_at(layer, h + 1):
                        make_bias(layer, m)
                    if layer == 0 and h < 4 * MOD_CHUNKS:
                        i, k = h // 4, h % 4
                        w = raw[:, place["mod_g", i] % RAW, :, :]
                        acc = acc_g[:, i % 2, :]
                        scalar = v[:, V_CACT + k:V_CACT + k + 1]
                        if k == 0:
                            wait_raw(pool, ("mod_g", i))
                            if i >= 2:
                                pool.wait_ge(mod_T, 3 + i)
                            nc.gpsimd.tensor_scalar(acc, w[:, 0, :], scalar, 0.0, ALU.mult, ALU.add).then_inc(pool_step, 2)
                            pool.wait_ge(pool_step, 9 * i + 2)
                        else:
                            nc.gpsimd.tensor_scalar(w[:, k, :], w[:, k, :], scalar, 0.0, ALU.mult, ALU.add).then_inc(pool_step, 1)
                            pool.wait_ge(pool_step, 9 * i + 2 * k + 1)
                            nc.gpsimd.tensor_tensor(acc, acc, w[:, k, :], ALU.add).then_inc(pool_step, 1)
                        if k == 3:
                            pool.wait_ge(pool_step, 9 * i + 8)
                            pool.wait_ge(mod_part, i + 1)
                            nc.gpsimd.tensor_tensor(acc, acc, acc_v[:, :], ALU.add).then_inc(pool_step, 1)

        @block.tensor
        def _(pe):
            def mm(o, a, b, start, stop):
                return nc.tensor.matmul(o, a, b, start=start, stop=stop, skip_group_check=True)

            def mm3(o, a_hi, a_lo, b_hi, b_lo, start, stop):
                mm(o, a_hi, b_hi, start, False)
                mm(o, a_hi, b_lo, False, False)
                return mm(o, a_lo, b_hi, False, stop)

            def mod_columns(acc, layer, i):
                for f in range(4):
                    o = 32 * layer + 4 * i + f
                    s = mm(small[:, o:o + 1], acc[:, f * P:(f + 1) * P], v[:, V_EPS + 1:V_EPS + 2], True, True)
                s.then_inc(mod_T, 1)

            pe.wait_ge(cst_in, 16)
            pe.wait_ge(vec_in, 16)
            nc.tensor.transpose(small[:, P:P + P], rows[:, :], ident).then_inc(cols_T, 1)
            pe.wait_ge(x_in, 16)
            for i in range(4):
                if i >= 2:
                    pe.wait_ge(xT_ok, i - 1)
                for a in range(2):
                    for t in range(2):
                        s = nc.tensor.transpose(proj[i % 2][:, a * S + t * P:a * S + (t + 1) * P],
                                                x_tok[:, t, (2 * i + a) * P:(2 * i + a + 1) * P], ident)
                s.then_inc(xT_T, 1)
            pe.wait_ge(cols_ok, 1)
            for i in range(4):
                pe.wait_ge(mod_v, i + 1)
                mod_columns(acc_v, 0, i)

            def mean_squares(j, kind):
                pe.wait_ge(late_in, 16)
                if j:
                    pe.wait_ge(nt_ok, j)
                pe.wait_ge(sq_ok, SQUARED[j])
                ones = head_mean if kind == "unit" else mean128
                mm(sumsq[:, :], ones, n_sq[:, :], True, True).then_inc(ssq_ok, 1)

            def turn(layer, m, t):
                M = 16 * layer + m
                pe.wait_ge(prob_ok, M + 1)
                if t:
                    pe.wait_ge(probsT_ok, t)
                for b in range(3):
                    s = nc.tensor.transpose(turned[:, b * P:(b + 1) * P], probs[:, M % 3, b * P:(b + 1) * P], ident)
                s.then_inc(turn_ok, 1)

            def mix(layer, m, t):
                grp, wide = m // 8, layer == 0 and m < 8
                hh = m % 8
                if wide:
                    o, f = mixed[:, :], slice(P * (hh // 2), P * (hh // 2) + P)
                else:
                    o, f = mixed[HD * (hh % 2):HD * (hh % 2) + HD, :], slice(HD * hh, HD * hh + HD)
                if wide or m % 2 == 0:
                    pe.wait_ge(y_raw, 8 * layer + m // 2)
                mm(o[:, 0:S], val[:, grp, 0, f], probsT[:, t % 2, 0:S], True, False)
                mm(o[:, P:S], val[:, grp, 1, f], probsT[:, t % 2, S:MAPW], False, True).then_inc(pv_ok, 1)

            def scores(layer, m):
                M = 16 * layer + m
                grp, hh = m // 8, m % 8
                if m % 8 == 0:
                    pe.wait_ge(norm_ok, max(j for j in UNIT_NORMS if NORMS[j][0] == layer and NORMS[j][3] // 6 == grp) + 1)
                if M >= 2:
                    pe.wait_ge(logit_ok, M - 1)
                q, k = qZ[:, grp, hh, :], kT[:, grp, hh // 2, :]
                mm(score[M % 2][:, 0:P], q[:, 0:P], k[:, 0:P], True, True)
                mm(score[M % 2][:, P:MAPW], q[:, P:S], k[:, 0:S], True, True).then_inc(score_ok, 1)

            def stick_logits(m):
                if m == 0:
                    pe.wait_ge(free_act, frees(UNITS + 2 * Q2 + 1, False))
                    pe.wait_ge(masks_ok, 1)
                    pe.wait_ge(logit_ok, 24)
                    pe.wait_ge(probsT_ok, 20)
                if m >= 3:
                    pe.wait_ge(d_a, m - 2)
                q, k = qZ[:, 1, m, :], kT[:, 1, m // 2, :]
                mm(score[m % 3][:, 0:S], k[:, 0:P], q[:, 0:S], True, False)
                mm(score[m % 3][:, S:MAPW], k[:, P:S], q[:, P:S], False, False)
                mm(score[m % 3][:, 0:P], mask_id[:, :], mask_tri[:, :], False, False)
                mm(score[m % 3][:, S:MAPW], mask_id[:, :], mask_tri[:, :], False, False).then_inc(score_ok, 1)

            def stick_sums(m):
                pe.wait_ge(d_sp, m + 1)
                sp = probs[:, m % 3, :]
                mm(score[m % 3][:, 0:MAPW], tri, sp[:, 0:MAPW], False, False)
                mm(score[m % 3][:, P:S], neg, sp[:, S:MAPW], False, True).then_inc(d_tri, 1)

            def project(layer, h):
                u, half = h // 2, h % 2
                n = UNITS * layer + u
                piece = SLOTS * layer + h
                b, wh, wl = proj[n % 2], w_hi[:, piece % PIECES, :, :], w_lo[:, piece % PIECES, :, :]
                pe.wait_ge(lo_done, piece + 1)
                if half == 0 and n >= 2:
                    if freed_by_vector(n - 2):
                        pe.wait_ge(free_dve, frees(n - 2, True))
                    else:
                        pe.wait_ge(free_act, frees(n - 2, False))
                parts = ((0, 1), (2, 3)) if u in (0, IN_UNITS) else ((0, 1, 2, 3),)
                for kks in parts:
                    for side in range(2):
                        o = b[:, side * UNIT:(side + 1) * UNIT]
                        f = slice(side * P, (side + 1) * P)
                        for kk in kks:
                            k = 4 * half + kk
                            start, stop = k == 0 and side == 0, k == KB - 1
                            if u >= IN_UNITS:
                                if u == IN_UNITS and side == 0:
                                    pe.wait_ge(y_lo_ok, 4 * layer + k // 2 + 1)
                                s = mm3(o, wh[:, kk, f], wl[:, kk, f], y_hi[:, k, :], y_lo[:, k, :], start, stop)
                            elif u // 2 in (V1, V2):
                                s = mm3(o, h_hi[:, k, f], h_lo[:, k, f], wh[:, kk, :], wl[:, kk, :], start, stop)
                            else:
                                if u == 0 and side == 0:
                                    pe.wait_ge(h_ok, KB * layer + k + 1)
                                s = mm3(o, wh[:, kk, f], wl[:, kk, f], h_hi[:, k, :], h_lo[:, k, :], start, stop)
                s.then_inc(half_done, 1)

            def attend(layer, h):
                for j, kind, _ in norm_at(layer, h):
                    mean_squares(j, kind)
                for m in maps_at(layer, h, 1):
                    t = head_of(layer, m)
                    if t is not None:
                        turn(layer, m, t)
                for m in maps_at(layer, h, 2):
                    t = head_of(layer, m)
                    if t is not None:
                        pe.wait_ge(probsT_ok, t + 1)
                        if m % 8 == (1 if layer == 0 and m < 8 else 0):
                            pe.wait_ge(free_act, frees(UNITS * layer + 2 * (V1 if m < 8 else V2) + 1, False))
                        mix(layer, m, t)
                for m in sticks_at(layer, h, TRI_LAG):
                    stick_sums(m)
                for m in sticks_at(layer, h, PV_LAG_D):
                    pe.wait_ge(d_a, m + 1)
                    if m == 0:
                        pe.wait_ge(free_act, frees(UNITS + 2 * V2 + 1, False))
                    mix(1, 8 + m, 20 + m)
                for m in maps_at(layer, h):
                    scores(layer, m)
                for m in sticks_at(layer, h):
                    stick_logits(m)
                if layer == 0:
                    for i in range(8):
                        if h == 4 * i + MOD_LAG:
                            pe.wait_ge(pool_step, 9 * (i + 1))
                            pe.wait_ge(mod_ok, 1 if i < 2 else 2)
                            if i < 2:
                                mod_columns(acc_g[:, i % 2, :], 0, 4 + i)
                            else:
                                mod_columns(acc_g[:, i % 2, :], 1, i - 2)

            for layer in range(LAYERS):
                j = norm_at(layer, -1)[0][0]
                if j:
                    pe.wait_ge(nt_ok, j)
                for k in range(KB):
                    if k % 2 == 0:
                        pe.wait_ge(xsq, 4 * layer + k // 2 + 1)
                    s = mm(sumsq[:, 0:S], mean, gates[:, k, :], k == 0, k == KB - 1)
                s.then_inc(ssq_ok, 1)
                for h in range(SLOTS):
                    if h < 2 * IN_UNITS:
                        project(layer, h)
                        attend(layer, h)
                    else:
                        attend(layer, h)
                        project(layer, h)
            for i in range(4):
                t, half = i % 2, i // 2
                pe.wait_ge(free_dve, frees(UNITS * LAYERS - 3 + 2 * half, True))
                for f in range(4):
                    s = nc.tensor.transpose(final[i][:, f * P:(f + 1) * P],
                                            xT[:, 4 * half + f, t * P:(t + 1) * P], ident)
                s.then_inc(out_T, 1)


def constants():
    import numpy as np
    p, col = np.arange(P)[:, None], np.arange(S)[None, :]
    d = P + p - col
    count = sum(((d % dil == 0) & (d <= window)).astype(int) for window, dil in ((128, 1), (512, 4), (2048, 16)))
    inside = (d >= 0) & (count > 0)
    f = np.arange(P)[None, :]
    parts = [p == f, np.full((P, P), 1.0 / D), (p // HD == f // HD) / HD, np.full((P, P), 1.0 / P),
             -1.0 * (p >= f), np.full((P, P), -1.0),
             d, np.where(d >= 0, 0.0, MASKED), np.where(inside, -np.log(np.maximum(count, 1)), MASKED)]
    return np.concatenate([np.asarray(a, np.float32) for a in parts], axis=1)


def small_vectors(inputs):
    import numpy as np
    rows = [np.reshape(inputs[name], (-1, P)) for name in ("c", "norm_w", "b_mod")]
    rows += [np.concatenate([inputs[f"{g}_{qk}_norm"]] * 2, axis=1) for g in "abc" for qk in "qk"]
    rows += [inputs["a_subln"]]
    used = np.concatenate(rows, axis=0)
    return np.concatenate([used, np.zeros((P - len(used), P), used.dtype)], axis=0)


def kernel(**inputs):
    import numpy as np
    import concourse.bacc as bacc
    from concourse.bass_utils import run_bass_kernel_spmd

    nc = bacc.Bacc("TRN2", target_bir_lowering=False, num_devices=1)
    arrays = {f"in_{name}": np.ascontiguousarray(inputs[name]) for name in ("x", "w_mod", "w_in", "w_out", "a_lambda")}
    arrays["in_vectors"] = small_vectors({name: np.asarray(a) for name, a in inputs.items()})
    arrays["in_constants"] = constants()
    args = [nc.dram_tensor(name, a.shape, mybir.dt.from_np(a.dtype), kind="ExternalInput").ap()
            for name, a in arrays.items()]
    out = nc.dram_tensor("out_x", (1, S, D), F32, kind="ExternalOutput").ap()
    program(nc, *args, out)
    return run_bass_kernel_spmd(nc, [arrays], core_ids=[0]).results[0]["out_x"]
```

```python
import math
from contextlib import ExitStack

import concourse.bass as bass
from concourse import mybir

F32 = mybir.dt.float32
F32R = mybir.dt.float32r
BF16 = mybir.dt.bfloat16
ALU = mybir.AluOpType
ACT = mybir.ActivationFunctionType

P = 128
D = 1024
S = 256
LAYERS = 2
KB = D // P
HD = 64
EPS = 1e-6
SCALE = HD ** -0.5
MASKED = 1e30
LAMBDA_INIT = 0.8 - 0.6 * math.exp(-0.3 * 0)
CHUNK = 512
UNIT = 256
KH = KB // 2
RAW = 6
PIECES = 3
AHEAD = 2
MAPW = 384

IN_UNITS = 16
UNITS = 20
SLOTS = 2 * UNITS
CHUNKS = UNITS // 2
ORDER = (1, 0, 2, 5, 4, 6, 3, 7)
K1, Q1, V1, K2, Q2, V2, G1, G2 = range(8)
FIRST_MAP = (11, 23)
FIRST_D = 21
TURN_LAG, PV_LAG = 2, 3
TRI_LAG, PV_LAG_D = 2, 3
MAPS = 24
TURNED = 20
GATE_AT = (26, 28, 30, 32)
SUBLN_AT = (24, 26)

MOD_AT = {(0, 2 + 3 * g // 2): divmod(g, 4) for g in range(24)}
MOD_AT.update({(1, 4 + 2 * g): divmod(24 + g, 4) for g in range(8)})
MOD_SUM_LAG = 2
MOD_SUM_AT = {(layer, h + MOD_SUM_LAG): i for (layer, h), (i, step) in MOD_AT.items() if step == 3}
MOD_PE = (3, 7)

R_C, R_NORM, R_BMOD = 0, KB, KB + LAYERS * KB
R_QK = R_BMOD + LAYERS * 3 * KB
R_SUBLN = R_QK + 6
ROWS = R_SUBLN + 1

C_ID, C_MEAN, C_HEAD, C_MEAN128, C_TRI, C_NEG = (P * i for i in range(6))
C_DIST, C_CAUSAL, C_DIL = (P * 6 + S * i for i in range(3))
C_LATE = 2 * P
CONSTS = P * 6 + S * 3

V_A, V_B, V_GATE = 0, 2 * KB, 4 * KB
V_QK = 6 * KB
V_SUBLN = V_QK + 6
V_CACT = V_SUBLN + 1
V_TMP = V_CACT + KB
V_LAM = V_TMP + 8
V_EPS = V_LAM + 8
V_N = V_EPS + 2


def work(h):
    if 0 <= h - 2 * IN_UNITS < 4:
        return IN_UNITS + h % 2, (h - 2 * IN_UNITS) // 2
    return h // 2, h % 2


def lo_first(layer, h):
    return h >= 2 * IN_UNITS or h % 2 == 1 and h < 24


def stored_at(h):
    return [h - (SLOTS - 4)] if SLOTS - 4 <= h < SLOTS - 1 else []


def done(n):
    return SLOTS * (n // UNITS) + next(h for h in range(SLOTS) if work(h) == (n % UNITS, 1)) + 1


def maps_at(layer, h, lag=0):
    out = []
    for m in range(16 if layer == 0 else 8):
        if h == FIRST_MAP[m // 8] + m % 8 + lag - (m == 15 and lag == PV_LAG):
            out.append(m)
    return out


def sticks_at(layer, h, lag=0):
    h -= lag
    return [h - FIRST_D] if layer == 1 and 0 <= h - FIRST_D < 8 else []


def head_of(layer, m):
    if layer == 0 and m < 8:
        return m // 2 if m % 2 else None
    return m - 4 if layer == 0 else 12 + m


def normed(layer, u):
    return u < IN_UNITS and u // 2 in ((K1, Q1, K2, Q2) if layer == 0 else (K1, Q1))


def norms():
    out = []
    for layer in range(LAYERS):
        out.append((layer, -1, "rms", 0))
        for h in range(SLOTS):
            if h % 2 and h >= 3 and normed(layer, (h - 3) // 2):
                out.append((layer, h, "unit", (h - 3) // 2))
            if layer == 0 and h in SUBLN_AT:
                out.append((layer, h, "subln", SUBLN_AT.index(h)))
    return out


NORMS = norms()


def norm_at(layer, h):
    return [(j, kind, i) for j, (la, hh, kind, i) in enumerate(NORMS) if (la, hh) == (layer, h)]


def freed_by_vector(n):
    u = n % UNITS
    return u // 2 in (G1, G2) or u >= IN_UNITS


def frees(n, vector):
    return sum(freed_by_vector(i) == vector for i in range(n + 1))


SQUARED = [sum(kind != "rms" for _, _, kind, _ in NORMS[:j + 1]) for j in range(len(NORMS))]
UNIT_NORMS = [j for j, (_, _, kind, _) in enumerate(NORMS) if kind == "unit"]


def turned_by(layer, m):
    return m // 2 + 1 if layer == 0 and m < 8 else (m - 3 if layer == 0 else 13 + m)


def slope(layer, m):
    if layer == 0 and m < 8:
        return 2.0 ** (-8.0 * (m // 2 + 1) / 4)
    return 2.0 ** (-(m % 8 + 1))


def program(nc, x, w_mod, w_in, w_out, a_lambda, vectors, consts, out):
    with ExitStack() as ctx:
        def sb(name, shape, dt=F32):
            return ctx.enter_context(nc.sbuf_tensor(name, shape, dt))

        def bank(name):
            return ctx.enter_context(nc.psum_tensor(name, [P, 512], F32))

        def sem(name):
            return ctx.enter_context(nc.semaphore(name))

        raw = sb("raw", [P, RAW, KH, CHUNK])
        w_hi = sb("w_hi", [P, PIECES, KH, UNIT], F32R)
        w_lo = sb("w_lo", [P, PIECES, KH, UNIT], F32R)
        h_hi = sb("h_hi", [P, KB, S], F32R)
        h_lo = sb("h_lo", [P, KB, S], F32R)
        y_hi = sb("y_hi", [P, KB, S], F32R)
        y_lo = sb("y_lo", [P, KB, S], F32R)
        xT = sb("xT", [P, KB, S])
        y = sb("y", [P, KB, S])
        gates = sb("gates", [P, KB, S])
        kT = sb("kT", [P, 2, 4, S])
        qZ = sb("qZ", [P, 2, 8, S])
        val = sb("val", [P, 2, 2, CHUNK])
        n_raw = sb("n_raw", [P, 2, 512])
        n_sq = sb("n_sq", [P, 512])
        part_hi = sb("part_hi", [P, 2 * MAPW], F32R)
        part_lo = sb("part_lo", [P, 2 * MAPW], F32R)
        exact = sb("exact", [P, 4, P], F32R)
        n_y0 = sb("n_y0", [P, 512])
        n_t = sb("n_t", [P, 512])
        logits = sb("logits", [P, 2, 512])
        probs = sb("probs", [P, 3, 512])
        probsT = sb("probsT", [P, 2, 512])
        bias = sb("bias", [P, 2, S])
        lam = logits[:, 0, 0:4 * HD].rearrange("p (i d) -> p i d", i=4)
        acc_v = sb("acc_v", [P, CHUNK])
        acc_g = sb("acc_g", [P, 2, CHUNK])
        x_sum = acc_g[:, 0, 0:S]
        rows = sb("rows", [P, P])
        cols = sb("cols", [P, ROWS])
        v = sb("v", [P, V_N])
        cst = sb("cst", [P, CONSTS])
        mask_id = sb("mask_id", [P, P], BF16)
        mask_tri = sb("mask_tri", [P, P], BF16)
        stat = sb("stat", [P, 2, 8])

        dist, causal, dilated = (cst[:, o:o + S] for o in (C_DIST, C_CAUSAL, C_DIL))
        ident, mean, tri = (cst[:, o:o + P] for o in (C_ID, C_MEAN, C_TRI))
        head_mean_r, mean128_r, tri_r, neg_r = (exact[:, i, :] for i in range(4))
        sq_hi, sq_lo = part_hi[:, 0:512], part_lo[:, 0:512]
        sp_hi, sp_lo = ([t[:, i * MAPW:(i + 1) * MAPW] for i in range(2)] for t in (part_hi, part_lo))
        x_tok = y[:, :, :].rearrange("p a b -> p (a b)").rearrange("p (t f) -> p t f", t=2)
        out_tok = x_tok

        proj = [bank("proj0"), bank("proj1")]
        sumsq = bank("sumsq")
        score = [bank("score0"), bank("score1"), bank("turned")]
        turned = score[2]
        mixed = bank("mixed")
        final = score + [mixed]
        small = bank("small")

        def bank_of(n):
            u = n % UNITS
            return sumsq if u == IN_UNITS + 1 else proj[u % 2 if u < IN_UNITS + 2 else u - IN_UNITS - 2]

        raw_full = [sem(f"raw_full{i}") for i in range(RAW)]
        w_first = sem("w_first")
        x_in, vec_in, lam_in = sem("x_in"), sem("vec_in"), sem("lam_in")
        cst_in, late_in = sem("cst_in"), sem("late_in")
        masks_ok = sem("masks_ok")
        exact_ok = sem("exact_ok")
        zeroed = sem("zeroed")
        cols_T, cols_ok = sem("cols_T"), sem("cols_ok")
        act_c = sem("act_c")
        vec_c = sem("vec_c")
        xT_T, xT_ok = sem("xT_T"), sem("xT_ok")
        mod_v = sem("mod_v")
        mod_pe = sem("mod_pe")
        mod_part = sem("mod_part")
        pool_step = sem("pool_step")
        mod_T = sem("mod_T")
        scale_ok = sem("scale_ok")
        mod_ok = sem("mod_ok")
        hi_done, lo_done = sem("hi_done"), sem("lo_done")
        half_done = sem("half_done")
        free_act, free_dve = sem("free_act"), sem("free_dve")
        xsq, xsum = sem("xsq"), sem("xsum")
        x_rms, x_normed = sem("x_rms"), sem("x_normed")
        h_pre, h_hi_ok, h_ok = sem("h_pre"), sem("h_hi_ok"), sem("h_ok")
        sq_full, sq_hi_ok, sq_ok = sem("sq_full"), sem("sq_hi_ok"), sem("sq_ok")
        ssq_ok = sem("ssq_ok")
        ln_ok, y0_ok, y0_sq = (sem(n) for n in ("ln_ok", "y0_ok", "y0_sq"))
        nt_ok, norm_ok = sem("nt_ok"), sem("norm_ok")
        g_step, ln_sigmoid = sem("g_step"), sem("ln_sigmoid")
        slope_ok, bias_ok = sem("slope_ok"), sem("bias_ok")
        score_ok, logit_ok, exp_ok, prob_ok = (sem(n) for n in ("score_ok", "logit_ok", "exp_ok", "prob_ok"))
        turn_ok, probsT_ok = sem("turn_ok"), sem("probsT_ok")
        pv_ok, y_raw = sem("pv_ok"), sem("y_raw")
        d_abs, d_exp, d_ln, d_sp = (sem(n) for n in ("d_abs", "d_exp", "d_ln", "d_sp"))
        sp_full_hi, sp_ok, d_tri, d_a = (sem(n) for n in ("sp_full_hi", "sp_ok", "d_tri", "d_a"))
        y_ok, y_hi_ok, y_lo_ok = sem("y_ok"), sem("y_hi_ok"), sem("y_lo_ok")
        out_T, out_ok, stored = sem("out_T"), sem("out_ok"), sem("stored")
        dve_step = sem("dve_step")

        chunks = [("mod_v", i) for i in range(4)] + [("w", 0)]
        needed = {("w", i): 4 * i - AHEAD for i in range(1, CHUNKS * LAYERS)}
        needed.update({("mod_g", i): SLOTS * layer + h for (layer, h), (i, step) in MOD_AT.items() if step == 0})
        chunks += sorted(needed, key=lambda key: (needed[key], key[0] != "w"))
        halves = [(kind, i, half) for kind, i in chunks for half in range(2)]
        place = {key: n for n, key in enumerate(halves)}

        def source(kind, i, half):
            if kind == "mod_v":
                w, col = w_mod[0], CHUNK * ((i + 2) % 4)
            elif kind == "mod_g":
                w, col = (w_mod[0], CHUNK * (4 + i)) if i < 2 else (w_mod[1], CHUNK * (i - 2))
            elif i % CHUNKS < IN_UNITS // 2:
                w, col = w_in[i // CHUNKS], CHUNK * ORDER[i % CHUNKS]
            else:
                w, col = w_out[i // CHUNKS], CHUNK * (i % CHUNKS - IN_UNITS // 2)
            return w[half * KH * P:(half + 1) * KH * P, col:col + CHUNK].rearrange("(k p) n -> p k n", p=P)

        def raw_block(kind, i, k):
            return raw[:, place[kind, i, k // KH] % RAW, k % KH, :]

        def raw_piece(piece):
            u, half = work(piece % SLOTS)
            chunk = CHUNKS * (piece // SLOTS) + u // 2
            return raw[:, place["w", chunk, half] % RAW, :, (u % 2) * UNIT:(u % 2 + 1) * UNIT]

        def wait_raw(eng, kind, i, half):
            n = place[kind, i, half]
            eng.wait_ge(raw_full[n % RAW], 16 * (n // RAW + 1))

        block = ctx.enter_context(nc.Block())

        @block.sync
        def _(sp):
            def load(n):
                if n >= RAW:
                    was, j, half = halves[n - RAW]
                    if was == "mod_v":
                        sp.wait_ge(mod_v, 2 * j + 1 + half)
                        sp.wait_ge(mod_pe, 2 * j + 1 + half)
                    elif was == "mod_g":
                        sp.wait_ge(pool_step, 9 * j + (4, 9)[half])
                        sp.wait_ge(mod_part, 2 * j + 1 + half)
                    else:
                        last = max(p for p in range(4) if work(4 * (j % CHUNKS) + p)[1] == half)
                        sp.wait_ge(lo_done, 4 * j + last + 1)
                to, whence = raw[:, n % RAW, :, :], source(*halves[n])
                if halves[n] == ("w", 0, 0):
                    sp.dma_start(to[:, :, 0:UNIT], whence[:, :, 0:UNIT]).then_inc(w_first, 16)
                    sp.dma_start(to[:, :, UNIT:], whence[:, :, UNIT:]).then_inc(raw_full[n % RAW], 16)
                else:
                    sp.dma_start(to, whence).then_inc(raw_full[n % RAW], 16)

            sp.dma_start(rows[:, :], vectors).then_inc(vec_in, 16)
            sp.dma_start(lam, a_lambda.rearrange("a i d -> a (i d)").broadcast_to([P, 4 * HD])
                         .rearrange("p (i d) -> p i d", i=4)).then_inc(lam_in, 16)
            sp.dma_start(cst[:, 0:C_LATE], consts[:, 0:C_LATE]).then_inc(cst_in, 16)
            sp.dma_start(x_tok, x[0].rearrange("(t p) f -> p t f", p=P)).then_inc(x_in, 16)
            for n in range(len(halves)):
                load(n)
                if halves[n] == ("w", 1, 1):
                    sp.dma_start(cst[:, C_LATE:], consts[:, C_LATE:]).then_inc(late_in, 16)
            for i in range(4):
                sp.wait_ge(out_ok, i + 1)
                sp.dma_start(out[0, :, i * UNIT:(i + 1) * UNIT].rearrange("(t p) f -> p t f", p=P),
                             out_tok[:, :, i * UNIT:(i + 1) * UNIT]).then_inc(stored, 16)
            sp.wait_ge(stored, 64)

        @block.scalar
        def _(act):
            act.preload_act_table_set("natural_log_exp_and_others")
            act.wait_ge(cols_ok, 1)
            nc.scalar.activation(v[:, V_CACT:V_CACT + KB], cols[:, R_C:R_C + KB], ACT.Exp, scale=-1.0).then_inc(act_c, 1)
            act.wait_ge(vec_c, 1)
            nc.scalar.activation(v[:, V_LAM + 2:V_LAM + 4], v[:, V_LAM:V_LAM + 2], ACT.Exp).then_inc(act_c, 1)

            for i in range(4):
                act.wait_ge(xT_T, i + 1)
                nc.scalar.activation(xT[:, 2 * i:2 * i + 2, :], proj[i % 2][:, :], ACT.Copy).then_inc(xT_ok, 1)

            def split_hi(piece):
                if piece:
                    wait_raw(act, "w", piece // 4, work(piece % SLOTS)[1])
                else:
                    act.wait_ge(w_first, 16)
                if piece >= PIECES:
                    act.wait_ge(half_done, piece - PIECES + 1)
                nc.scalar.activation(w_hi[:, piece % PIECES, :, :], raw_piece(piece), ACT.Copy).then_inc(hi_done, 1)

            def norm_seed(j, width):
                act.wait_ge(ssq_ok, j + 1)
                if j:
                    act.wait_ge(norm_ok, j)
                nc.scalar.activation(n_y0[:, 0:width], sumsq[:, 0:width], ACT.Ln,
                                     bias=v[:, V_EPS:V_EPS + 1]).then_inc(ln_ok, 1)
                act.wait_ge(ln_ok, j + 1)
                nc.scalar.activation(n_y0[:, 0:width], n_y0[:, 0:width], ACT.Exp, scale=-0.5).then_inc(y0_ok, 1)
                act.wait_ge(y0_ok, j + 1)
                nc.scalar.activation(n_t[:, 0:width], n_y0[:, 0:width], ACT.Square).then_inc(y0_sq, 1)

            def take_unit(layer, u):
                n = UNITS * layer + u
                group, part = u // 2, u % 2
                b = proj[n % 2]
                act.wait_ge(half_done, done(n))
                if normed(layer, u):
                    r = UNIT_NORMS.index(norm_of[layer, u])
                    if r >= 2:
                        act.wait_ge(norm_ok, UNIT_NORMS[r - 2] + 1)
                    nc.scalar.activation(n_raw[:, r % 2, :], b[:, :], ACT.Copy).then_inc(free_act, 1)
                elif group in (V1, V2):
                    nc.scalar.activation(val[:, int(group == V2), :, part * UNIT:(part + 1) * UNIT],
                                         b[:, :].rearrange("p (t n) -> p t n", t=2), ACT.Copy).then_inc(free_act, 1)
                elif group == K2:
                    nc.scalar.activation(kT[:, 1, 2 * part:2 * part + 2, :],
                                         b[:, :].rearrange("p (a s) -> p a s", a=2), ACT.Copy).then_inc(free_act, 1)
                elif group == Q2:
                    act.wait_ge(zeroed, 4)
                    for odd in range(2):
                        half = slice(HD * odd, HD * odd + HD)
                        i = nc.scalar.activation(qZ[half, 1, 4 * part + odd:4 * part + 4:2, :],
                                                 b[half, :].rearrange("p (a s) -> p a s", a=2), ACT.Copy, scale=SCALE)
                    i.then_inc(free_act, 1)
                else:
                    i = 2 * (group - G1) + part
                    act.wait_ge(h_ok, KB * (layer + 1))
                    nc.scalar.activation(gates[:, 2 * i:2 * i + 2, :],
                                         b[:, :].rearrange("p (a s) -> p a s", a=2), ACT.Abs).then_inc(g_step, 1)
                    g, steps = gates[:, 2 * i:2 * i + 2, :], 4 * (4 * layer + i)
                    act.wait_ge(g_step, steps + 1)
                    nc.scalar.activation(g, g, ACT.Exp, scale=-1.0).then_inc(g_step, 1)
                    act.wait_ge(g_step, steps + 2)
                    nc.scalar.activation(g, g, ACT.Ln, bias=1.0).then_inc(g_step, 1)

            def take_gates(layer, i):
                g = gates[:, 2 * i:2 * i + 2, :]
                act.wait_ge(ln_sigmoid, 4 * layer + i + 1)
                nc.scalar.activation(g, g, ACT.Exp).then_inc(g_step, 1)

            def square_x(layer, i):
                if layer:
                    act.wait_ge(free_dve, frees(UNITS * layer - 4 + i, True))
                    act.wait_ge(y_ok, 4 * layer)
                else:
                    act.wait_ge(xT_ok, i + 1)
                nc.scalar.activation(gates[:, 2 * i:2 * i + 2, :], xT[:, 2 * i:2 * i + 2, :], ACT.Square).then_inc(xsq, 1)

            def square_hi(layer, j, kind, i):
                if j > 1:
                    act.wait_ge(ssq_ok, j)
                if kind == "unit":
                    act.wait_ge(free_act, frees(UNITS * layer + i, False))
                    src = n_raw[:, UNIT_NORMS.index(j) % 2, :]
                else:
                    act.wait_ge(y_raw, 2 * i + 2)
                    src = y[:, 2 * i:2 * i + 2, :].rearrange("p a s -> p (a s)")
                nc.scalar.activation(sq_hi, src, ACT.Square).then_inc(sq_hi_ok, 1)

            def store_x(i):
                act.wait_ge(out_T, i + 1)
                act.wait_ge(y_lo_ok, 4 * LAYERS)
                nc.scalar.activation(out_tok[:, :, i * UNIT:(i + 1) * UNIT],
                                     final[i][:, :].rearrange("p (t f) -> p t f", t=2), ACT.Copy).then_inc(out_ok, 1)

            norm_of = {(la, i): j for j, (la, _, kind, i) in enumerate(NORMS) if kind == "unit"}

            for layer in range(LAYERS):
                for i in range(4) if layer == 0 else (3,):
                    square_x(layer, i)
                norm_seed(norm_at(layer, -1)[0][0], S)
                for k in range(KB):
                    if layer == 0 and k % KH == 0:
                        split_hi(k // KH)
                    act.wait_ge(h_pre, KB * layer + k + 1)
                    act.wait_ge(mod_ok, 1)
                    nc.scalar.activation(h_hi[:, k, :], gates[:, k, :], ACT.Identity,
                                         bias=v[:, V_B + KB * layer + k:V_B + KB * layer + k + 1]).then_inc(h_hi_ok, 1)
                for h in range(SLOTS):
                    if SLOTS * layer + h + AHEAD < SLOTS * LAYERS:
                        split_hi(SLOTS * layer + h + AHEAD)
                    for j, kind, i in norm_at(layer, h + 1):
                        square_hi(layer, j, kind, i)
                    if h % 2 and h < 2 * IN_UNITS:
                        take_unit(layer, h // 2)
                    if h % 2 == 0 and 2 * G1 < h // 2 <= IN_UNITS:
                        take_gates(layer, h // 2 - 1 - 2 * G1)
                    if layer == 0 and h == 1:
                        act.wait_ge(late_in, 16)
                        nc.scalar.activation(exact[:, :, :], cst[:, C_HEAD:C_NEG + P].rearrange("p (a b) -> p a b", a=4),
                                             ACT.Copy).then_inc(exact_ok, 1)
                    for j, _, _ in norm_at(layer, h):
                        norm_seed(j, 512)
                    for m in maps_at(layer, h, TURN_LAG):
                        t = head_of(layer, m)
                        if t is not None:
                            act.wait_ge(turn_ok, t + 1)
                            if t >= 2:
                                act.wait_ge(pv_ok, t - 1)
                            nc.scalar.activation(probsT[:, t % 2, 0:MAPW], turned[:, 0:MAPW], ACT.Copy).then_inc(probsT_ok, 1)
                    for m in maps_at(layer, h, PV_LAG):
                        t = head_of(layer, m)
                        if t is not None and (layer == 0 and m < 8 or m % 2):
                            blk = m // 2
                            act.wait_ge(pv_ok, t + 1)
                            nc.scalar.activation(y[:, blk, :], mixed[:, 0:S], ACT.Copy).then_inc(y_raw, 1)
                    for m in sticks_at(layer, h, TRI_LAG):
                        act.wait_ge(d_tri, m + 1)
                        act.wait_ge(pv_ok, TURNED + m - 1)
                        nc.scalar.activation(probsT[:, m % 2, 0:MAPW], score[m % 3][:, 0:MAPW], ACT.Exp).then_inc(d_a, 1)
                    for m in sticks_at(layer, h, PV_LAG_D):
                        if m % 2:
                            act.wait_ge(pv_ok, TURNED + m + 1)
                            nc.scalar.activation(y[:, 4 + m // 2, :], mixed[:, 0:S], ACT.Copy).then_inc(y_raw, 1)
                    for m in maps_at(layer, h):
                        M = 16 * layer + m
                        act.wait_ge(logit_ok, M + 1)
                        if M >= 2:
                            act.wait_ge(prob_ok, M - 1)
                        if M >= 3:
                            act.wait_ge(turn_ok, turned_by((M - 3) // 16, (M - 3) % 16))
                        for tile, cs in enumerate((slice(0, P), slice(P, MAPW))):
                            i = nc.scalar.activation(probs[:, M % 3, cs], logits[:, M % 2, cs], ACT.Exp, scale=-1.0,
                                                     bias=stat[:, M % 2, tile:tile + 1],
                                                     accum_out=stat[:, M % 2, 2 + tile:3 + tile])
                        i.then_inc(exp_ok, 1)
                    for m in sticks_at(layer, h):
                        act.wait_ge(score_ok, MAPS + m + 1)
                        if m >= 2:
                            act.wait_ge(d_sp, m - 1)
                        else:
                            act.wait_ge(prob_ok, MAPS)
                        nc.scalar.activation(logits[:, m % 2, 0:MAPW], score[m % 3][:, 0:MAPW], ACT.Abs).then_inc(d_abs, 1)
                        act.wait_ge(d_abs, m + 1)
                        nc.scalar.activation(logits[:, m % 2, 0:MAPW], logits[:, m % 2, 0:MAPW], ACT.Exp, scale=-1.0).then_inc(d_exp, 1)
                        act.wait_ge(d_exp, m + 1)
                        nc.scalar.activation(logits[:, m % 2, 0:MAPW], logits[:, m % 2, 0:MAPW], ACT.Ln, bias=1.0).then_inc(d_ln, 1)
                    if layer < LAYERS - 1 and h > 2 * IN_UNITS and work(h - 1)[1]:
                        square_x(layer + 1, work(h - 1)[0] - IN_UNITS)
                    if h in GATE_AT:
                        i = GATE_AT.index(h)
                        act.wait_ge(y_ok, 4 * layer + i + 1)
                        nc.scalar.activation(y_hi[:, 2 * i:2 * i + 2, :], y[:, 2 * i:2 * i + 2, :], ACT.Copy).then_inc(y_hi_ok, 1)
                    if layer == LAYERS - 1:
                        for i in stored_at(h):
                            store_x(i)
            store_x(3)

        @block.vector
        def _(dve):
            steps = [0]

            def link(ins):
                steps[0] += 1
                ins.then_inc(dve_step, 1)
                dve.wait_ge(dve_step, steps[0])

            def col(i, n=1):
                return v[:, i:i + n]

            nc.vector.memset(col(V_EPS), EPS)
            nc.vector.memset(col(V_EPS + 1), 1.0)

            dve.wait_ge(cols_T, 1)
            nc.vector.tensor_copy(cols[:, :], small[:, P:P + ROWS]).then_inc(cols_ok, 1)
            dve.wait_ge(lam_in, 16)
            for i in range(2):
                j = nc.vector.tensor_tensor_reduce(out=n_t[:, 0:HD], in0=lam[:, 2 * i, :], in1=lam[:, 2 * i + 1, :],
                                                   scale=1.0, scalar=0.0, op0=ALU.mult, op1=ALU.add,
                                                   accum_out=col(V_LAM + i))
                if i == 0:
                    link(j)
            j.then_inc(vec_c, 1)
            dve.wait_ge(act_c, 1)
            dve.wait_ge(cols_ok, 1)
            link(nc.vector.tensor_scalar_add(col(V_CACT, KB), col(V_CACT, KB), 1.0))
            link(nc.vector.reciprocal(col(V_CACT, KB), col(V_CACT, KB)))
            nc.vector.tensor_tensor(col(V_CACT, KB), col(V_CACT, KB), cols[:, R_C:R_C + KB], ALU.mult).then_inc(vec_c, 1)
            dve.wait_ge(act_c, 2)
            nc.vector.scalar_tensor_tensor(out=col(V_LAM + 4), in0=col(V_LAM + 3), scalar=-LAMBDA_INIT,
                                           in1=col(V_LAM + 2), op0=ALU.add, op1=ALU.subtract)
            for i in range(6):
                f = 0.5 * SCALE if i % 2 == 0 else -0.5
                nc.vector.tensor_scalar_mul(col(V_QK + i), cols[:, R_QK + i:R_QK + i + 1], f)
            link(nc.vector.tensor_scalar_mul(col(V_SUBLN), cols[:, R_SUBLN:R_SUBLN + 1], -0.5 * (1.0 - LAMBDA_INIT)))

            def take_scale(layer, sums):
                b = R_BMOD + 3 * KB * layer
                nw = R_NORM + KB * layer
                link(nc.vector.tensor_tensor(col(V_TMP, KB), sums, cols[:, b + KB:b + 2 * KB], ALU.add))
                link(nc.vector.scalar_tensor_tensor(out=col(V_TMP, KB), in0=col(V_TMP, KB), scalar=1.0,
                                                    in1=cols[:, nw:nw + KB], op0=ALU.add, op1=ALU.mult))
                return nc.vector.tensor_scalar_mul(col(V_A + KB * layer, KB), col(V_TMP, KB), -0.5)

            def take_shift(layer, sums):
                b = R_BMOD + 3 * KB * layer
                return nc.vector.tensor_tensor(col(V_B + KB * layer, KB), sums, cols[:, b:b + KB], ALU.add)

            def take_gate(layer):
                o = 32 * layer + 2 * KB
                b = R_BMOD + 3 * KB * layer + 2 * KB
                return nc.vector.tensor_tensor(col(V_GATE + KB * layer, KB), small[:, o:o + KB],
                                               cols[:, b:b + KB], ALU.add)

            def split_lo(piece):
                dve.wait_ge(hi_done, piece + 1)
                nc.vector.tensor_tensor(w_lo[:, piece % PIECES, :, :], raw_piece(piece),
                                        w_hi[:, piece % PIECES, :, :], ALU.subtract).then_inc(lo_done, 1)

            def refine(j, width, signal=None):
                dve.wait_ge(y0_sq, j + 1)
                nc.vector.scalar_tensor_tensor(out=n_t[:, 0:width], in0=sumsq[:, 0:width], scalar=EPS,
                                               in1=n_t[:, 0:width], op0=ALU.add, op1=ALU.mult).then_inc(nt_ok, 1)
                dve.wait_ge(nt_ok, j + 1)
                i = nc.vector.scalar_tensor_tensor(out=n_t[:, 0:width], in0=n_t[:, 0:width], scalar=-3.0,
                                                   in1=n_y0[:, 0:width], op0=ALU.add, op1=ALU.mult)
                if signal is None:
                    link(i)
                else:
                    i.then_inc(signal, 1)

            dve.wait_ge(vec_c, 2)
            for i in range(4):
                acc = acc_g[:, i % 2, :]
                if i >= 2:
                    dve.wait_ge(mod_T, i - 1)
                blocks = [k for k in range(KB) if k not in MOD_PE]
                for k in blocks:
                    if k % KH == 0:
                        wait_raw(dve, "mod_v", i, k // KH)
                    w = raw_block("mod_v", i, k)
                    if k == 0:
                        j = nc.vector.tensor_scalar_mul(acc, w, col(V_CACT))
                    else:
                        j = nc.vector.scalar_tensor_tensor(out=acc, in0=w, scalar=col(V_CACT + k),
                                                           in1=acc, op0=ALU.mult, op1=ALU.add)
                    if k + 1 in MOD_PE:
                        j.then_inc(mod_v, 1)
                        dve.wait_ge(mod_v, 2 * i + 1 + k // KH)
                    else:
                        link(j)
                    if i == 3 and k == KH - 2:
                        dve.wait_ge(mod_T, 2)
                        take_scale(0, mixed[:, 0:KB]).then_inc(scale_ok, 1)
                if i == 1:
                    refine(0, S, x_rms)

            split_lo(0)
            dve.wait_ge(mod_T, 4)
            take_shift(0, small[:, 0:KB]).then_inc(mod_ok, 1)
            dve.wait_ge(mod_ok, 1)

            def norm_unit(j, layer, u):
                refine(j, 512)
                r = UNIT_NORMS.index(j)
                grp, part = u // 6, u % 2
                is_k = u // 2 in (K1, K2)
                w = V_QK + 4 * layer + 2 * grp + is_k
                if is_k:
                    i = nc.vector.scalar_tensor_tensor(
                        out=kT[:, grp, 2 * part:2 * part + 2, :],
                        in0=n_raw[:, r % 2, :].rearrange("p (a s) -> p a s", a=2), scalar=col(w),
                        in1=n_t[:, :].rearrange("p (a s) -> p a s", a=2), op0=ALU.mult, op1=ALU.mult)
                else:
                    dve.wait_ge(zeroed, 4)
                    for odd in range(2):
                        half = slice(HD * odd, HD * odd + HD)
                        i = nc.vector.scalar_tensor_tensor(
                            out=qZ[half, grp, 4 * part + odd:4 * part + 4:2, :],
                            in0=n_raw[half, r % 2, :].rearrange("p (a s) -> p a s", a=2), scalar=v[half, w:w + 1],
                            in1=n_t[half, :].rearrange("p (a s) -> p a s", a=2), op0=ALU.mult, op1=ALU.mult)
                i.then_inc(norm_ok, 1)

            def norm_subln(j, i):
                refine(j, 512)
                nc.vector.scalar_tensor_tensor(
                    out=y[:, 2 * i:2 * i + 2, :], in0=y[:, 2 * i:2 * i + 2, :], scalar=col(V_SUBLN),
                    in1=n_t[:, :].rearrange("p (a s) -> p a s", a=2), op0=ALU.mult, op1=ALU.mult).then_inc(norm_ok, 1)

            for layer in range(LAYERS):
                if layer:
                    refine(norm_at(layer, -1)[0][0], S)
                for k in range(KB + 1):
                    if layer == 0 and k == KH:
                        split_lo(1)
                    if layer and k < KB:
                        nc.vector.scalar_tensor_tensor(
                            out=gates[:, k, :], in0=xT[:, k, :], scalar=col(V_A + KB * layer + k),
                            in1=n_t[:, 0:S], op0=ALU.mult, op1=ALU.mult).then_inc(h_pre, 1)
                    if k:
                        dve.wait_ge(h_hi_ok, KB * layer + k)
                        nc.vector.scalar_tensor_tensor(
                            out=h_lo[:, k - 1, :], in0=gates[:, k - 1, :], scalar=col(V_B + KB * layer + k - 1),
                            in1=h_hi[:, k - 1, :], op0=ALU.add, op1=ALU.subtract).then_inc(h_ok, 1)
                dve.wait_ge(h_ok, KB * (layer + 1))
                nc.vector.tensor_copy(col(V_TMP), col(V_EPS)).then_inc(norm_ok, 1)
                if layer:
                    nc.vector.tensor_scalar_mul(mask_id[:, :], ident, MASKED)
                    nc.vector.tensor_copy(mask_tri[:, :], tri).then_inc(masks_ok, 1)
                for h in range(SLOTS):
                    u = h // 2
                    n = UNITS * layer + u
                    for j, kind, i in norm_at(layer, h - 1) if h else []:
                        if kind == "unit":
                            norm_unit(j, layer, i)
                        else:
                            norm_subln(j, i)
                    if lo_first(layer, h) and SLOTS * layer + h + AHEAD < SLOTS * LAYERS:
                        split_lo(SLOTS * layer + h + AHEAD)
                    if h % 2 == 0 and 2 * G1 < u <= IN_UNITS:
                        i = u - 1 - 2 * G1
                        g = gates[:, 2 * i:2 * i + 2, :]
                        dve.wait_ge(g_step, 4 * (4 * layer + i) + 4)
                        nc.vector.tensor_tensor(g, proj[(n - 1) % 2][:, :].rearrange("p (a s) -> p a s", a=2), g,
                                                ALU.mult).then_inc(free_dve, 1)
                        dve.wait_ge(free_dve, frees(n - 1, True))
                    if h >= 2 * IN_UNITS and work(h)[1]:
                        i = work(h)[0] - IN_UNITS
                        dve.wait_ge(half_done, SLOTS * layer + h + 1)
                        for fb in range(2):
                            k = 2 * i + fb
                            s = nc.vector.scalar_tensor_tensor(
                                out=xT[:, k, :], in0=bank_of(UNITS * layer + IN_UNITS + i)[:, fb * S:(fb + 1) * S],
                                scalar=col(V_GATE + KB * layer + k), in1=xT[:, k, :], op0=ALU.mult, op1=ALU.add)
                        s.then_inc(free_dve, 1)
                    for m in maps_at(layer, h):
                        M = 16 * layer + m
                        dve.wait_ge(score_ok, M + 1)
                        dve.wait_ge(bias_ok, M + 1)
                        if M >= 2:
                            dve.wait_ge(exp_ok, M - 1)
                        for tile, (cs, bs) in enumerate(((slice(0, P), slice(P, S)), (slice(P, MAPW), slice(0, S)))):
                            i = nc.vector.tensor_tensor_reduce(
                                out=logits[:, M % 2, cs], in0=score[M % 2][:, cs], in1=bias[:, M % 2, bs],
                                scale=1.0, scalar=3e38, op0=ALU.add, op1=ALU.min,
                                accum_out=stat[:, M % 2, tile:tile + 1])
                        i.then_inc(logit_ok, 1)
                    if h in GATE_AT:
                        i = GATE_AT.index(h)
                        ys = y[:, 2 * i:2 * i + 2, :]
                        dve.wait_ge(y_raw, 8 * layer + 2 * i + 2)
                        nc.vector.tensor_tensor(ys, ys, gates[:, 2 * i:2 * i + 2, :], ALU.mult).then_inc(y_ok, 1)
                    if not lo_first(layer, h) and SLOTS * layer + h + AHEAD < SLOTS * LAYERS:
                        split_lo(SLOTS * layer + h + AHEAD)
                    if h % 2 and u < IN_UNITS and u // 2 in (G1, G2):
                        i = u - 2 * G1
                        g = gates[:, 2 * i:2 * i + 2, :]
                        dve.wait_ge(g_step, 4 * (4 * layer + i) + 3)
                        nc.vector.scalar_tensor_tensor(
                            out=g, in0=proj[n % 2][:, :].rearrange("p (a s) -> p a s", a=2), scalar=0.0, in1=g,
                            op0=ALU.min, op1=ALU.subtract).then_inc(ln_sigmoid, 1)
                    if (layer, h) in MOD_AT:
                        i, step = MOD_AT[layer, h]
                        k = KH * (step // 2) + 2 + step % 2
                        w = raw_block("mod_g", i, k)
                        if step % 2 == 0:
                            wait_raw(dve, "mod_g", i, step // 2)
                        if step == 0:
                            if i:
                                dve.wait_ge(pool_step, 9 * i)
                            j = nc.vector.tensor_scalar_mul(acc_v[:, :], w, col(V_CACT + k))
                        else:
                            j = nc.vector.scalar_tensor_tensor(out=acc_v[:, :], in0=w, scalar=col(V_CACT + k),
                                                               in1=acc_v[:, :], op0=ALU.mult, op1=ALU.add)
                        if step % 2 == 0:
                            link(j)
                        else:
                            j.then_inc(mod_part, 1)
                            dve.wait_ge(mod_part, 2 * i + 1 + step // 2)
                    for m in maps_at(layer, h):
                        M = 16 * layer + m
                        dve.wait_ge(exp_ok, M + 1)
                        st = stat[:, M % 2, :]
                        link(nc.vector.reciprocal(st[:, 4:6], st[:, 2:4]))
                        for tile, cs in enumerate((slice(0, P), slice(P, MAPW))):
                            if layer == 0 and m < 8 and m % 2:
                                if tile == 0:
                                    link(nc.vector.tensor_scalar_mul(st[:, 6:8], st[:, 4:6], col(V_LAM + 4)))
                                i = nc.vector.scalar_tensor_tensor(
                                    out=probs[:, M % 3, cs], in0=probs[:, M % 3, cs], scalar=st[:, 6 + tile:7 + tile],
                                    in1=probs[:, (M - 1) % 3, cs], op0=ALU.mult, op1=ALU.add)
                            else:
                                i = nc.vector.tensor_scalar_mul(probs[:, M % 3, cs], probs[:, M % 3, cs],
                                                                st[:, 4 + tile:5 + tile])
                        i.then_inc(prob_ok, 1)
                        dve.wait_ge(prob_ok, M + 1)
                    for m in sticks_at(layer, h):
                        dve.wait_ge(d_ln, m + 1)
                        if m >= 3:
                            dve.wait_ge(d_tri, m - 2)
                        else:
                            dve.wait_ge(turn_ok, TURNED)
                        nc.vector.scalar_tensor_tensor(
                            out=probs[:, m % 3, 0:MAPW], in0=score[m % 3][:, 0:MAPW], scalar=0.0,
                            in1=logits[:, m % 2, 0:MAPW], op0=ALU.max, op1=ALU.add).then_inc(d_sp, 1)
                    if h in GATE_AT:
                        i = GATE_AT.index(h)
                        dve.wait_ge(y_hi_ok, 4 * layer + i + 1)
                        nc.vector.tensor_tensor(y_lo[:, 2 * i:2 * i + 2, :], y[:, 2 * i:2 * i + 2, :],
                                                y_hi[:, 2 * i:2 * i + 2, :], ALU.subtract).then_inc(y_lo_ok, 1)
                    i = MOD_SUM_AT.get((layer, h))
                    if i in (1, 5, 7):
                        dve.wait_ge(mod_T, 5 + i)
                        if i == 5:
                            take_shift(1, small[:, 32:32 + KB])
                            take_scale(1, small[:, 32 + KB:32 + 2 * KB]).then_inc(mod_ok, 1)
                        else:
                            take_gate(layer).then_inc(mod_ok, 1)
                        dve.wait_ge(mod_ok, 2 + (1, 5, 7).index(i))

        @block.gpsimd
        def _(pool):
            for grp in range(2):
                for odd in range(2):
                    nc.gpsimd.memset(qZ[HD * (1 - odd):HD * (2 - odd), grp, odd::2, :], 0.0).then_inc(zeroed, 1)
                    pool.wait_ge(zeroed, 2 * grp + odd + 1)

            def square(layer, h):
                for j, kind, i in norm_at(layer, h):
                    if kind == "unit":
                        pool.wait_ge(free_act, frees(UNITS * layer + i, False))
                        src = n_raw[:, UNIT_NORMS.index(j) % 2, :]
                    else:
                        pool.wait_ge(y_raw, 2 * i + 2)
                        src = y[:, 2 * i:2 * i + 2, :].rearrange("p a s -> p (a s)")
                    nc.gpsimd.tensor_tensor(n_sq[:, :], src, src, ALU.mult).then_inc(sq_full, 1)
                    pool.wait_ge(sq_full, SQUARED[j])
                    pool.wait_ge(sq_hi_ok, SQUARED[j])
                    nc.gpsimd.tensor_tensor(sq_lo, n_sq[:, :], sq_hi, ALU.subtract).then_inc(sq_ok, 1)
                    pool.wait_ge(sq_ok, SQUARED[j])

            def split_softplus(m):
                pool.wait_ge(d_sp, m + 1)
                if m >= 2:
                    pool.wait_ge(d_tri, m - 1)
                else:
                    pool.wait_ge(ssq_ok, len(NORMS))
                sp = probs[:, m % 3, 0:MAPW]
                nc.gpsimd.tensor_copy(sp_hi[m % 2], sp).then_inc(sp_full_hi, 1)
                pool.wait_ge(sp_full_hi, m + 1)
                nc.gpsimd.tensor_tensor(sp_lo[m % 2], sp, sp_hi[m % 2], ALU.subtract).then_inc(sp_ok, 1)

            def make_bias(layer, m):
                M = 16 * layer + m
                if M >= 2:
                    pool.wait_ge(logit_ok, M - 1)
                mask = dilated if layer == 0 and m >= 8 else causal
                nc.gpsimd.tensor_scalar(bias[:, M % 2, :], dist, slope(layer, m), 0.0, ALU.mult, ALU.add).then_inc(slope_ok, 1)
                pool.wait_ge(slope_ok, M + 1)
                nc.gpsimd.tensor_tensor(bias[:, M % 2, :], bias[:, M % 2, :], mask, ALU.add).then_inc(bias_ok, 1)

            pool.wait_ge(x_rms, 1)
            pool.wait_ge(xT_ok, 4)
            pool.wait_ge(nt_ok, 1)
            for k in range(KB):
                nc.gpsimd.tensor_tensor(gates[:, k, :], xT[:, k, :], n_t[:, 0:S], ALU.mult).then_inc(x_normed, 1)
            pool.wait_ge(scale_ok, 1)
            for k in range(KB):
                pool.wait_ge(x_normed, k + 1)
                nc.gpsimd.tensor_scalar(gates[:, k, :], gates[:, k, :], v[:, V_A + k:V_A + k + 1], 0.0,
                                        ALU.mult, ALU.add).then_inc(h_pre, 1)
            pool.wait_ge(late_in, 16)
            for layer in range(LAYERS):
                for h in range(SLOTS):
                    square(layer, h + 1)
                    for m in maps_at(layer, h + 1):
                        make_bias(layer, m)
                    if (layer, h) in MOD_AT:
                        i, step = MOD_AT[layer, h]
                        k = KH * (step // 2) + step % 2
                        w = raw_block("mod_g", i, k)
                        acc = acc_g[:, i % 2, :]
                        scalar = v[:, V_CACT + k:V_CACT + k + 1]
                        if step % 2 == 0:
                            wait_raw(pool, "mod_g", i, step // 2)
                        if step == 0:
                            pool.wait_ge(mod_T, 3 + i)
                            nc.gpsimd.tensor_scalar(acc, w, scalar, 0.0, ALU.mult, ALU.add).then_inc(pool_step, 2)
                            pool.wait_ge(pool_step, 9 * i + 2)
                        else:
                            nc.gpsimd.tensor_scalar(w, w, scalar, 0.0, ALU.mult, ALU.add).then_inc(pool_step, 1)
                            pool.wait_ge(pool_step, 9 * i + 2 * step + 1)
                            nc.gpsimd.tensor_tensor(acc, acc, w, ALU.add).then_inc(pool_step, 1)
                        if step == 3:
                            pool.wait_ge(pool_step, 9 * i + 8)
                            pool.wait_ge(mod_part, 2 * i + 2)
                            nc.gpsimd.tensor_tensor(acc, acc, acc_v[:, :], ALU.add).then_inc(pool_step, 1)
                    for m in sticks_at(layer, h):
                        split_softplus(m)
                if layer < LAYERS - 1:
                    pool.wait_ge(mod_T, 4 + 5)
                    for k in range(1, KB - 2):
                        pool.wait_ge(xsq, 4 * (layer + 1) + k // 2 + 1)
                        so_far = gates[:, 0, :] if k == 1 else x_sum
                        nc.gpsimd.tensor_tensor(x_sum, so_far, gates[:, k, :], ALU.add).then_inc(xsum, 1)
                        pool.wait_ge(xsum, k)
                    pool.wait_ge(ssq_ok, norm_at(layer + 1, -1)[0][0] + 1)

        @block.tensor
        def _(pe):
            def mm(o, a, b, start, stop):
                return nc.tensor.matmul(o, a, b, start=start, stop=stop, skip_group_check=True)

            def mm3(o, a_hi, a_lo, b_hi, b_lo, start, stop):
                mm(o, a_hi, b_hi, start, False)
                mm(o, a_hi, b_lo, False, False)
                return mm(o, a_lo, b_hi, False, stop)

            def mod_columns(acc, sums, start=True):
                for f in range(4):
                    s = mm(sums[:, f:f + 1], acc[:, f * P:(f + 1) * P], v[:, V_EPS + 1:V_EPS + 2], start, True)
                s.then_inc(mod_T, 1)

            def x_mean_squares(layer):
                if layer:
                    pe.wait_ge(nt_ok, norm_at(layer, -1)[0][0])
                    pe.wait_ge(free_dve, frees(UNITS * layer - 3, True))
                    pe.wait_ge(xsum, KB - 3)
                    mm(sumsq[:, 0:S], mean, x_sum, True, False)
                for k in range(KB - 2 if layer else 0, KB):
                    if k % 2 == 0:
                        pe.wait_ge(xsq, 4 * layer + k // 2 + 1)
                    s = mm(sumsq[:, 0:S], mean, gates[:, k, :], k == 0, k == KB - 1)
                s.then_inc(ssq_ok, 1)

            pe.wait_ge(cst_in, 16)
            pe.wait_ge(vec_in, 16)
            nc.tensor.transpose(small[:, P:P + P], rows[:, :], ident).then_inc(cols_T, 1)
            pe.wait_ge(x_in, 16)
            for i in range(4):
                if i >= 2:
                    pe.wait_ge(xT_ok, i - 1)
                for a in range(2):
                    for t in range(2):
                        s = nc.tensor.transpose(proj[i % 2][:, a * S + t * P:a * S + (t + 1) * P],
                                                x_tok[:, t, (2 * i + a) * P:(2 * i + a + 1) * P], ident)
                s.then_inc(xT_T, 1)
            pe.wait_ge(cols_ok, 1)
            pe.wait_ge(vec_c, 2)
            sums = [bank[:, 4 * i:4 * i + 4] for bank in (mixed, small) for i in range(2)]
            for i in range(4):
                for half, k in enumerate(MOD_PE):
                    if half and i:
                        pe.wait_ge(mod_v, 2 * i)
                        mod_columns(acc_g[:, (i - 1) % 2, :], sums[i - 1], start=False)
                    wait_raw(pe, "mod_v", i, half)
                    for f in range(4):
                        j = mm(sums[i][:, f:f + 1], raw_block("mod_v", i, k)[:, f * P:(f + 1) * P],
                               v[:, V_CACT + k:V_CACT + k + 1], i % 2 == 0 and half == 0 and f == 0, False)
                    j.then_inc(mod_pe, 1)
                if i == 0:
                    x_mean_squares(0)
            pe.wait_ge(mod_v, 8)
            mod_columns(acc_g[:, 1, :], sums[3], start=False)

            def mean_squares(j, kind):
                pe.wait_ge(exact_ok, 1)
                if j:
                    pe.wait_ge(nt_ok, j)
                pe.wait_ge(sq_ok, SQUARED[j])
                ones = head_mean_r if kind == "unit" else mean128_r
                mm(sumsq[:, :], ones, sq_hi, True, False)
                mm(sumsq[:, :], ones, sq_lo, False, True).then_inc(ssq_ok, 1)

            def turn(layer, m, t):
                M = 16 * layer + m
                pe.wait_ge(prob_ok, M + 1)
                if t:
                    pe.wait_ge(probsT_ok, t)
                for b in range(3):
                    s = nc.tensor.transpose(turned[:, b * P:(b + 1) * P], probs[:, M % 3, b * P:(b + 1) * P], ident)
                s.then_inc(turn_ok, 1)

            def mix(layer, m, t):
                grp, wide = m // 8, layer == 0 and m < 8
                hh = m % 8
                if wide:
                    o, f = mixed[:, :], slice(P * (hh // 2), P * (hh // 2) + P)
                else:
                    o, f = mixed[HD * (hh % 2):HD * (hh % 2) + HD, :], slice(HD * hh, HD * hh + HD)
                if wide or m % 2 == 0:
                    pe.wait_ge(y_raw, 8 * layer + m // 2)
                mm(o[:, 0:S], val[:, grp, 0, f], probsT[:, t % 2, 0:S], True, False)
                mm(o[:, P:S], val[:, grp, 1, f], probsT[:, t % 2, S:MAPW], False, True).then_inc(pv_ok, 1)

            def scores(layer, m):
                M = 16 * layer + m
                grp, hh = m // 8, m % 8
                if m % 8 == 0:
                    pe.wait_ge(norm_ok, max(j for j in UNIT_NORMS if NORMS[j][0] == layer and NORMS[j][3] // 6 == grp) + 1)
                if M >= 2:
                    pe.wait_ge(logit_ok, M - 1)
                q, k = qZ[:, grp, hh, :], kT[:, grp, hh // 2, :]
                mm(score[M % 2][:, 0:P], q[:, 0:P], k[:, 0:P], True, True)
                mm(score[M % 2][:, P:MAPW], q[:, P:S], k[:, 0:S], True, True).then_inc(score_ok, 1)

            def stick_logits(m):
                if m == 0:
                    pe.wait_ge(free_act, frees(UNITS + 2 * Q2 + 1, False))
                    pe.wait_ge(masks_ok, 1)
                    pe.wait_ge(logit_ok, MAPS)
                    pe.wait_ge(probsT_ok, TURNED)
                if m >= 3:
                    pe.wait_ge(d_a, m - 2)
                q, k = qZ[:, 1, m, :], kT[:, 1, m // 2, :]
                mm(score[m % 3][:, 0:S], k[:, 0:P], q[:, 0:S], True, False)
                mm(score[m % 3][:, S:MAPW], k[:, P:S], q[:, P:S], False, False)
                mm(score[m % 3][:, 0:P], mask_id[:, :], mask_tri[:, :], False, False)
                mm(score[m % 3][:, S:MAPW], mask_id[:, :], mask_tri[:, :], False, False).then_inc(score_ok, 1)

            def stick_sums(m):
                pe.wait_ge(sp_ok, m + 1)
                for part in (sp_hi[m % 2], sp_lo[m % 2]):
                    mm(score[m % 3][:, 0:MAPW], tri_r, part, False, False)
                    s = mm(score[m % 3][:, P:S], neg_r, part[:, S:MAPW], False, part is sp_lo[m % 2])
                s.then_inc(d_tri, 1)

            def project(layer, h):
                u, half = work(h)
                n = UNITS * layer + u
                piece = SLOTS * layer + h
                b, wh, wl = bank_of(n), w_hi[:, piece % PIECES, :, :], w_lo[:, piece % PIECES, :, :]
                pe.wait_ge(lo_done, piece + 1)
                if half == 0 and u == IN_UNITS + 1:
                    pe.wait_ge(nt_ok, sum(la <= layer for la, _, _, _ in NORMS))
                elif half == 0 and n >= 2:
                    was = IN_UNITS - 1 + UNITS * layer if u == IN_UNITS + 3 else n - 2
                    if freed_by_vector(was):
                        pe.wait_ge(free_dve, frees(was, True))
                    else:
                        pe.wait_ge(free_act, frees(was, False))
                parts = ((0, 1), (2, 3)) if u in (0, IN_UNITS, IN_UNITS + 1) else ((0, 1, 2, 3),)
                for kks in parts:
                    for side in range(2):
                        o = b[:, side * UNIT:(side + 1) * UNIT]
                        f = slice(side * P, (side + 1) * P)
                        for kk in kks:
                            k = 4 * half + kk
                            start, stop = k == 0 and side == 0, k == KB - 1
                            if u >= IN_UNITS:
                                if u <= IN_UNITS + 1 and side == 0:
                                    pe.wait_ge(y_lo_ok, 4 * layer + k // 2 + 1)
                                s = mm3(o, wh[:, kk, f], wl[:, kk, f], y_hi[:, k, :], y_lo[:, k, :], start, stop)
                            elif u // 2 in (V1, V2):
                                s = mm3(o, h_hi[:, k, f], h_lo[:, k, f], wh[:, kk, :], wl[:, kk, :], start, stop)
                            else:
                                if u == 0 and side == 0:
                                    pe.wait_ge(h_ok, KB * layer + k + 1)
                                s = mm3(o, wh[:, kk, f], wl[:, kk, f], h_hi[:, k, :], h_lo[:, k, :], start, stop)
                s.then_inc(half_done, 1)

            def attend(layer, h):
                for j, kind, _ in norm_at(layer, h):
                    mean_squares(j, kind)
                for m in maps_at(layer, h, TURN_LAG):
                    t = head_of(layer, m)
                    if t is not None:
                        turn(layer, m, t)
                for m in maps_at(layer, h, PV_LAG):
                    t = head_of(layer, m)
                    if t is not None:
                        pe.wait_ge(probsT_ok, t + 1)
                        if m % 8 == (1 if layer == 0 and m < 8 else 0):
                            pe.wait_ge(free_act, frees(UNITS * layer + 2 * (V1 if m < 8 else V2) + 1, False))
                        mix(layer, m, t)
                for m in sticks_at(layer, h, TRI_LAG):
                    stick_sums(m)
                for m in sticks_at(layer, h, PV_LAG_D):
                    pe.wait_ge(d_a, m + 1)
                    if m == 0:
                        pe.wait_ge(free_act, frees(UNITS + 2 * V2 + 1, False))
                    mix(1, 8 + m, TURNED + m)
                for m in maps_at(layer, h):
                    scores(layer, m)
                for m in sticks_at(layer, h):
                    stick_logits(m)
                i = MOD_SUM_AT.get((layer, h))
                if i is not None:
                    pe.wait_ge(pool_step, 9 * (i + 1))
                    pe.wait_ge(mod_ok, 1 if i < 2 else 2 if i < 6 else 3)
                    o = 4 * (4 + i) if i < 2 else 32 + 4 * (i - 2)
                    mod_columns(acc_g[:, i % 2, :], small[:, o:o + 4])

            def turn_x(i):
                pe.wait_ge(free_dve, frees(UNITS * LAYERS - 4 + i, True))
                for t in range(2):
                    for f in range(2):
                        s = nc.tensor.transpose(final[i][:, (2 * t + f) * P:(2 * t + f + 1) * P],
                                                xT[:, 2 * i + f, t * P:(t + 1) * P], ident)
                s.then_inc(out_T, 1)

            for layer in range(LAYERS):
                if layer:
                    x_mean_squares(layer)
                for h in range(SLOTS):
                    if h < 2 * IN_UNITS:
                        project(layer, h)
                        attend(layer, h)
                    else:
                        project(layer, h)
                        attend(layer, h)
                        if layer == LAYERS - 1:
                            for i in stored_at(h):
                                turn_x(i)
            turn_x(3)


def constants():
    import numpy as np
    p, col = np.arange(P)[:, None], np.arange(S)[None, :]
    d = P + p - col
    count = sum(((d % dil == 0) & (d <= window)).astype(int) for window, dil in ((128, 1), (512, 4), (2048, 16)))
    inside = (d >= 0) & (count > 0)
    f = np.arange(P)[None, :]
    parts = [p == f, np.full((P, P), 1.0 / D), (p // HD == f // HD) / HD, np.full((P, P), 1.0 / P),
             -1.0 * (p >= f), np.full((P, P), -1.0),
             d, np.where(d >= 0, 0.0, MASKED), np.where(inside, -np.log(np.maximum(count, 1)), MASKED)]
    return np.concatenate([np.asarray(a, np.float32) for a in parts], axis=1)


def small_vectors(inputs):
    import numpy as np
    rows = [np.reshape(inputs[name], (-1, P)) for name in ("c", "norm_w", "b_mod")]
    rows += [np.concatenate([inputs[f"{g}_{qk}_norm"]] * 2, axis=1) for g in "abc" for qk in "qk"]
    rows += [inputs["a_subln"]]
    used = np.concatenate(rows, axis=0)
    return np.concatenate([used, np.zeros((P - len(used), P), used.dtype)], axis=0)


def kernel(**inputs):
    import numpy as np
    import concourse.bacc as bacc
    from concourse.bass_utils import run_bass_kernel_spmd

    nc = bacc.Bacc("TRN2", target_bir_lowering=False, num_devices=1)
    arrays = {f"in_{name}": np.ascontiguousarray(inputs[name]) for name in ("x", "w_mod", "w_in", "w_out", "a_lambda")}
    arrays["in_vectors"] = small_vectors({name: np.asarray(a) for name, a in inputs.items()})
    arrays["in_constants"] = constants()
    args = [nc.dram_tensor(name, a.shape, mybir.dt.from_np(a.dtype), kind="ExternalInput").ap()
            for name, a in arrays.items()]
    out = nc.dram_tensor("out_x", (1, S, D), F32, kind="ExternalOutput").ap()
    program(nc, *args, out)
    return run_bass_kernel_spmd(nc, [arrays], core_ids=[0]).results[0]["out_x"]
```
